# Optimizing a Trainium2 kernel written in Bass

```python
import jax
import jax.numpy as jnp
from jax import lax
import numpy as np

D_MODEL = 1024
BATCH = 1
SEQ = 1024
DEPTH = 1
DEC_BATCH = 1
DEC_SEQ = 256
PAST_LEN = 128

GLA_HEADS = 4
GLA_DK = 64
GLA_DV = 128
GLA_GATE_RANK = 16
GLA_GATE_NORMALIZER = 16.0
GLA_CHUNK = 64
FNET_GROUPS = 4
FNET_GROUP_DIM = 128
PEER_HEADS = 8
PEER_NKEYS = 128
PEER_EXPERTS = PEER_NKEYS * PEER_NKEYS
PEER_QDIM = 256
PEER_TOPK = 16
PEER_TOKEN_BLOCK = 128
PLE_DIM = 256
LN_EPS = 1e-5
RMS_EPS = 1e-6
DEEPNORM_ALPHA = (2.0 * DEPTH) ** 0.25
DEEPNORM_BETA = (8.0 * DEPTH) ** -0.25

QK_WIDTH = GLA_HEADS * GLA_DK
V_WIDTH = GLA_HEADS * GLA_DV
F_WIDTH = FNET_GROUPS * FNET_GROUP_DIM
OFF_Q = 0
OFF_K = OFF_Q + QK_WIDTH
OFF_V = OFF_K + QK_WIDTH
OFF_R = OFF_V + V_WIDTH
OFF_AF = OFF_R + V_WIDTH
OFF_AB = OFF_AF + GLA_GATE_RANK
OFF_F = OFF_AB + GLA_GATE_RANK
IN_COLS = OFF_F + F_WIDTH

kernel_name = 'hybrid_gla_fnet_peer_encoder'

def layer_norm(x, g, b):
    xf = x.astype(jnp.float32)
    mu = jnp.mean(xf, axis=-1, keepdims=True)
    var = jnp.mean(jnp.square(xf - mu), axis=-1, keepdims=True)
    y = (xf - mu) * lax.rsqrt(var + LN_EPS) * g.astype(jnp.float32) + b.astype(jnp.float32)
    return y.astype(x.dtype)

def gla_one_direction(q, k, v, log_a, strict):
    bsz, nh, seq, dk = q.shape
    dv = v.shape[-1]
    c = GLA_CHUNK
    n = seq // c
    f32 = jnp.float32
    qc = q.astype(f32).reshape(bsz, nh, n, c, dk)
    kc = k.astype(f32).reshape(bsz, nh, n, c, dk)
    vc = v.astype(f32).reshape(bsz, nh, n, c, dv)
    bc = jnp.cumsum(log_a.astype(f32).reshape(bsz, nh, n, c, dk), axis=3)
    b_last = bc[:, :, :, c - 1:c, :]
    b_mid = bc[:, :, :, c // 2 - 1:c // 2, :]
    scores = jnp.einsum('bhncd,bhnsd->bhncs', qc * jnp.exp(bc - b_mid), kc * jnp.exp(b_mid - bc))
    mask = jnp.tril(jnp.ones((c, c), dtype=bool), k=-1 if strict else 0)
    scores = jnp.where(mask, scores, 0.0)
    o_intra = jnp.einsum('bhncs,bhnsv->bhncv', scores, vc)
    q_in = qc * jnp.exp(bc)
    k_st = kc * jnp.exp(b_last - bc)
    chunk_decay = jnp.exp(b_last[:, :, :, 0, :])

    def step(state, xs):
        q_n, k_n, v_n, d_n = xs
        o_n = jnp.einsum('bhcd,bhdv->bhcv', q_n, state)
        state = d_n[..., None] * state + jnp.einsum('bhcd,bhcv->bhdv', k_n, v_n)
        return state, o_n

    xs = (jnp.moveaxis(q_in, 2, 0), jnp.moveaxis(k_st, 2, 0),
          jnp.moveaxis(vc, 2, 0), jnp.moveaxis(chunk_decay, 2, 0))
    s0 = jnp.zeros((bsz, nh, dk, dv), f32)
    _, o_inter = lax.scan(step, s0, xs)
    o = o_intra + jnp.moveaxis(o_inter, 0, 2)
    return o.reshape(bsz, nh, seq, dv)

def token_mixer(x, w_in, w_af2, b_af, w_ab2, b_ab, gla_norm_g, w_ao, w_fo, w_mg, b_mg, w_o):
    bsz, seq, _ = x.shape
    f32 = jnp.float32
    h = x @ w_in

    def to_heads(t, d):
        return t.reshape(bsz, seq, GLA_HEADS, d).transpose(0, 2, 1, 3)

    q = to_heads(h[..., OFF_Q:OFF_K], GLA_DK) * (GLA_DK ** -0.5)
    k = to_heads(h[..., OFF_K:OFF_V], GLA_DK)
    v = to_heads(h[..., OFF_V:OFF_R], GLA_DV)
    r = h[..., OFF_R:OFF_AF]
    log_af = to_heads(jax.nn.log_sigmoid((h[..., OFF_AF:OFF_AB] @ w_af2 + b_af).astype(f32)) / GLA_GATE_NORMALIZER, GLA_DK)
    log_ab = to_heads(jax.nn.log_sigmoid((h[..., OFF_AB:OFF_F] @ w_ab2 + b_ab).astype(f32)) / GLA_GATE_NORMALIZER, GLA_DK)
    o_fwd = gla_one_direction(q, k, v, log_af, strict=False)
    rev = lambda t: jnp.flip(t, axis=2)
    o_bwd = rev(gla_one_direction(rev(q), rev(k), rev(v), rev(log_ab), strict=True))
    o = o_fwd + o_bwd
    o = o * lax.rsqrt(jnp.mean(jnp.square(o), axis=-1, keepdims=True) + RMS_EPS) * gla_norm_g.astype(f32)
    o = o.transpose(0, 2, 1, 3).reshape(bsz, seq, V_WIDTH).astype(x.dtype) * jax.nn.silu(r)
    branch_gla = o @ w_ao
    fg = h[..., OFF_F:IN_COLS].reshape(bsz, seq, FNET_GROUPS, FNET_GROUP_DIM).astype(f32)
    fr = jnp.real(jnp.fft.fft2(fg, axes=(1, 3), norm='ortho'))
    branch_fnet = fr.reshape(bsz, seq, F_WIDTH).astype(x.dtype) @ w_fo
    gates = jax.nn.sigmoid(x @ w_mg + b_mg)
    merged = gates[..., :D_MODEL] * branch_gla + gates[..., D_MODEL:] * branch_fnet
    return merged @ w_o

def peer_token_block(xb, w_pq, peer_keys, peer_u, peer_v):
    t = xb.shape[0]
    f32 = jnp.float32
    qh = (xb @ w_pq).reshape(t, PEER_HEADS, 2, PEER_QDIM // 2).astype(f32)
    s = jnp.einsum('thpc,hpkc->thpk', qh, peer_keys.astype(f32))
    s_top, i_top = lax.top_k(s, PEER_TOPK)
    cand = s_top[:, :, 0, :, None] + s_top[:, :, 1, None, :]
    cand_idx = i_top[:, :, 0, :, None] * PEER_NKEYS + i_top[:, :, 1, None, :]
    best, pos = lax.top_k(cand.reshape(t, PEER_HEADS, PEER_TOPK * PEER_TOPK), PEER_TOPK)
    idx = jnp.take_along_axis(cand_idx.reshape(t, PEER_HEADS, PEER_TOPK * PEER_TOPK), pos, axis=-1)
    g = jax.nn.softmax(best, axis=-1).reshape(t, PEER_HEADS * PEER_TOPK)
    idx = idx.reshape(t, PEER_HEADS * PEER_TOPK)
    u = peer_u[idx]
    a = jax.nn.gelu(jnp.einsum('td,ted->te', xb, u).astype(f32), approximate=False)
    w = (g * a).astype(xb.dtype)
    return jnp.einsum('te,ted->td', w, peer_v[idx])

def channel_mixer(x, w_pq, peer_keys, peer_u, peer_v):
    bsz, seq, d = x.shape
    xb = x.reshape(-1, PEER_TOKEN_BLOCK, d)
    out = lax.map(lambda blk: peer_token_block(blk, w_pq, peer_keys, peer_u, peer_v), xb)
    return out.reshape(bsz, seq, d)

def encoder_layer(x, p, w_in, w_af2, b_af, w_ab2, b_ab, gla_norm_g, w_ao, w_fo, w_mg, b_mg, w_o,
                  ln1_g, ln1_b, w_pq, peer_keys, peer_u, peer_v, w_pg, w_pe, ln2_g, ln2_b):
    mix = token_mixer(x, w_in, w_af2, b_af, w_ab2, b_ab, gla_norm_g, w_ao, w_fo, w_mg, b_mg, w_o)
    h = layer_norm(DEEPNORM_ALPHA * x + mix, ln1_g, ln1_b)
    ffn = channel_mixer(h, w_pq, peer_keys, peer_u, peer_v)
    ple = jax.nn.sigmoid(h @ w_pg) * (p.astype(h.dtype) @ w_pe)
    return layer_norm(DEEPNORM_ALPHA * h + ffn + ple, ln2_g, ln2_b)

def trunk(x, p, w_in, w_af2, b_af, w_ab2, b_ab, gla_norm_g, w_ao, w_fo, w_mg, b_mg, w_o,
          ln1_g, ln1_b, w_pq, peer_keys, peer_u, peer_v, w_pg, w_pe, ln2_g, ln2_b):
    for i in range(DEPTH):
        x = encoder_layer(x, p[i], w_in[i], w_af2[i], b_af[i], w_ab2[i], b_ab[i], gla_norm_g[i],
                          w_ao[i], w_fo[i], w_mg[i], b_mg[i], w_o[i], ln1_g[i], ln1_b[i],
                          w_pq[i], peer_keys[i], peer_u[i], peer_v[i], w_pg[i], w_pe[i],
                          ln2_g[i], ln2_b[i])
    return x

def setup_inputs(seed: int = 0) -> dict:
    key = jax.random.key(seed)
    ks = jax.random.split(key, 27)
    f32 = jnp.float32
    nrm = lambda k, shape, scale: jax.random.normal(k, shape, f32) * scale
    d = D_MODEL
    return {
        'x_prompt': nrm(ks[0], (BATCH, SEQ, d), 1.0),
        'x_sample': nrm(ks[1], (DEC_BATCH, DEC_SEQ, d), 1.0),
        'p_prompt': nrm(ks[2], (DEPTH, BATCH, SEQ, PLE_DIM), 1.0),
        'p_sample': nrm(ks[3], (DEPTH, DEC_BATCH, DEC_SEQ, PLE_DIM), 1.0),
        'w_in': nrm(ks[4], (DEPTH, d, IN_COLS), d ** -0.5),
        'w_af2': nrm(ks[5], (DEPTH, GLA_GATE_RANK, QK_WIDTH), GLA_GATE_RANK ** -0.5),
        'b_af': nrm(ks[6], (DEPTH, QK_WIDTH), 0.1),
        'w_ab2': nrm(ks[7], (DEPTH, GLA_GATE_RANK, QK_WIDTH), GLA_GATE_RANK ** -0.5),
        'b_ab': nrm(ks[8], (DEPTH, QK_WIDTH), 0.1),
        'gla_norm_g': 1.0 + nrm(ks[9], (DEPTH, GLA_DV), 0.02),
        'w_ao': nrm(ks[10], (DEPTH, V_WIDTH, d), V_WIDTH ** -0.5),
        'w_fo': nrm(ks[11], (DEPTH, F_WIDTH, d), F_WIDTH ** -0.5),
        'w_mg': nrm(ks[12], (DEPTH, d, 2 * d), d ** -0.5),
        'b_mg': nrm(ks[13], (DEPTH, 2 * d), 0.02),
        'w_o': nrm(ks[14], (DEPTH, d, d), DEEPNORM_BETA * d ** -0.5),
        'ln1_g': 1.0 + nrm(ks[15], (DEPTH, d), 0.02),
        'ln1_b': nrm(ks[16], (DEPTH, d), 0.02),
        'w_pq': nrm(ks[17], (DEPTH, d, PEER_HEADS * PEER_QDIM), d ** -0.5),
        'peer_keys': nrm(ks[18], (DEPTH, PEER_HEADS, 2, PEER_NKEYS, PEER_QDIM // 2), (PEER_QDIM // 2) ** -0.5),
        'peer_u': nrm(ks[19], (DEPTH, PEER_EXPERTS, d), d ** -0.5),
        'peer_v': nrm(ks[20], (DEPTH, PEER_EXPERTS, d), DEEPNORM_BETA),
        'w_pg': nrm(ks[21], (DEPTH, d, d), d ** -0.5),
        'w_pe': nrm(ks[22], (DEPTH, PLE_DIM, d), DEEPNORM_BETA * PLE_DIM ** -0.5),
        'ln2_g': 1.0 + nrm(ks[23], (DEPTH, d), 0.02),
        'ln2_b': nrm(ks[24], (DEPTH, d), 0.02),
    }

def reference(x_prompt, x_sample, p_prompt, p_sample, w_in, w_af2, b_af, w_ab2, b_ab, gla_norm_g,
              w_ao, w_fo, w_mg, b_mg, w_o, ln1_g, ln1_b, w_pq, peer_keys, peer_u, peer_v,
              w_pg, w_pe, ln2_g, ln2_b):
    y_prompt = trunk(x_prompt, p_prompt, w_in, w_af2, b_af, w_ab2, b_ab, gla_norm_g, w_ao, w_fo,
                     w_mg, b_mg, w_o, ln1_g, ln1_b, w_pq, peer_keys, peer_u, peer_v, w_pg, w_pe,
                     ln2_g, ln2_b)
    y_sample = trunk(x_sample, p_sample, w_in, w_af2, b_af, w_ab2, b_ab, gla_norm_g, w_ao, w_fo,
                     w_mg, b_mg, w_o, ln1_g, ln1_b, w_pq, peer_keys, peer_u, peer_v, w_pg, w_pe,
                     ln2_g, ln2_b)
    return (y_prompt, y_sample)


_drawn_inputs = setup_inputs


def setup_inputs(seed=0):
    import zlib

    import numpy as np

    out = dict(_drawn_inputs(seed))
    spreads = {}
    factors = {'b_af': 3.037,
     'b_ab': 3.08,
     'gla_norm_g': 3.555,
     'b_mg': 4.754,
     'ln2_g': 2.903,
     'ln2_b': 2.849}
    for name, (base, spread) in spreads.items():
        noise = np.random.default_rng([zlib.crc32(name.encode()), seed]).standard_normal(out[name].shape)
        drawn = base * np.exp(spread * noise) if base else spread * noise
        out[name] = jnp.asarray(drawn.astype(out[name].dtype))
    for name, factor in factors.items():
        out[name] = (out[name] * factor).astype(out[name].dtype)
    return out
```

```python
from contextlib import ExitStack

import concourse.bass as bass
import numpy as np
from concourse import mybir

f32 = mybir.dt.float32
f16 = mybir.dt.float16
u32 = mybir.dt.uint32
ALU = mybir.AluOpType
ACT = mybir.ActivationFunctionType
AX = mybir.AxisListType

P = 128
SEQS = (1024, 256)
NT = sum(SEQS)
TT = NT // P
BLOCKS = ((0, 512), (512, 512), (1024, 256))
NB = len(BLOCKS)
D = 1024
KO = D // P
HEADS, DK, DV, RANK, CHUNK = 4, 64, 128, 16, 64
NCH = NT // CHUNK
PAIRS = HEADS * DK // P
GROUPS, GDIM = 4, 128
PH, NKEYS, TOPK, HALF = 8, 128, 16, 128
HP = PH * 2
EXPERTS = NKEYS * NKEYS
GT = 2
DT = TT - GT
ND = DT * P
DENSE = tuple((t0, min(512, ND - t0)) for t0 in range(0, ND, 512))
PLE = 256
LN_EPS, RMS_EPS = 1e-5, 1e-6
ALPHA = 2.0 ** 0.25
WSCALE = 64.0
VSCALE = 4.0
GSCALE = 256.0
LOWEST = -3.0e38

M_Q, M_K, M_R, M_F, M_LOW, NM = 0, 2, 4, 8, 12, 13
AB_ROW = 32


def hi_lo(pe, out, lhs_hi, lhs_lo, rhs_hi, rhs_lo, first, last):
    pe.matmul(out, lhs_hi, rhs_hi, start=first, stop=False)
    pe.matmul(out, lhs_hi, rhs_lo, start=False, stop=False)
    return pe.matmul(out, lhs_lo, rhs_hi, start=False, stop=last)


def wait_apart(eng, sem, value):
    eng.wait_ge(sem, value)
    eng.nop(nofuse=True)


def project(nc, A, R):
    with ExitStack() as c:
        sb = lambda n, s, d: c.enter_context(nc.sbuf_tensor(n, s, d))
        sem = lambda n: R.stack.enter_context(nc.semaphore(n))
        x_hi, x_lo = sb("p_x_hi", [P, KO, NT], f16), sb("p_x_lo", [P, KO, NT], f16)
        x_st = sb("p_x_st", [P, 2, NT], f32)
        w_st = sb("p_w_st", [P, 2, D], f32)
        w_hi, w_lo = sb("p_w_hi", [P, 2, KO, P], f16), sb("p_w_lo", [P, 2, KO, P], f16)
        v_hi, v_lo = sb("p_v_hi", [P, KO, 512], f16), sb("p_v_lo", [P, KO, 512], f16)
        ps = c.enter_context(nc.psum_tensor("p_ps", [P, 2, 3, 512], f32))
        psv = c.enter_context(nc.psum_tensor("p_psv", [P, 2, 512], f32))
        x_in = [sem("p_x_in0"), sem("p_x_in1")]
        w_in = [sem("p_w_in0"), sem("p_w_in1")]
        x_hi_ok, x_lo_ok, w_hi_ok, w_lo_ok = sem("p_x_hi_ok"), sem("p_x_lo_ok"), sem("p_w_hi_ok"), sem("p_w_lo_ok")
        v_mm, v_ev, m_mm, m_ev, stored = sem("p_v_mm"), sem("p_v_ev"), sem("p_m_mm"), sem("p_m_ev"), sem("p_stored")
        NV = 4

        block = c.enter_context(nc.Block())

        @block.sync
        def _(sp):
            def load(s, slot, src):
                if isinstance(s, int) and s < 2:
                    pass
                else:
                    sp.wait_ge(w_lo_ok, s - 1)
                sp.dma_start(w_st[:, slot], src).then_inc(w_in[slot], 16)

            for k in range(KO):
                if k >= 2:
                    sp.wait_ge(x_lo_ok, k - 1)
                sp.dma_start(x_st[:, k % 2], A["x_t"][k]).then_inc(x_in[k % 2], 16)
                if k < 2:
                    load(k, k, A["w_v"][k])
            load(2, 0, A["w_v"][2])
            load(3, 1, A["w_v"][3])
            load(NV, 0, A["w_proj"][0])
            with sp.Fori(0, 6) as i:
                load(NV + 1 + 2 * i, 1, A["w_proj"][1 + 2 * i])
                load(NV + 2 + 2 * i, 0, A["w_proj"][2 + 2 * i])
            sp.wait_ge(x_hi_ok, KO)
            sp.wait_ge(x_lo_ok, KO)
            sp.dma_start(R.x_hi_dram, x_hi[:]).then_inc(stored, 16)
            sp.dma_start(R.x_lo_dram, x_lo[:]).then_inc(stored, 16)
            sp.wait_ge(stored, 32)

        def m_items(eng, body):
            body(eng, 0, 0, M_LOW, True)
            with eng.Fori(0, 6) as i:
                body(eng, 1 + 2 * i, 1, 2 * i, False)
                body(eng, 2 + 2 * i, 0, 2 * i + 1, False)

        @block.scalar
        def _(act):
            for k in range(KO):
                act.wait_ge(x_in[k % 2], 16 * (k // 2 + 1))
                act.activation(x_hi[:, k], x_st[:, k % 2], ACT.Copy).then_inc(x_hi_ok, 1)
                if k < 2:
                    act.wait_ge(w_in[k], 16)
                    act.activation(v_hi[:, 2 * k:2 * k + 2].rearrange("p a b -> p (a b)"), w_st[:, k],
                                   ACT.Copy, scale=WSCALE).then_inc(w_hi_ok, 1)
            for k in range(2, NV):
                act.wait_ge(w_in[k % 2], 32)
                act.activation(v_hi[:, 2 * k:2 * k + 2].rearrange("p a b -> p (a b)"), w_st[:, k % 2],
                               ACT.Copy, scale=WSCALE).then_inc(w_hi_ok, 1)

            def w_split(n, slot, nth):
                act.wait_ge(w_in[slot], 16 * nth)
                if not isinstance(n, int) or n >= 2:
                    act.wait_ge(m_mm, 3 * n - 3)
                act.activation(w_hi[:, slot].rearrange("p a b -> p (a b)"), w_st[:, slot], ACT.Copy,
                               scale=WSCALE).then_inc(w_hi_ok, 1)

            def evacuate(n, slot, m):
                for b, (t0, n_t) in enumerate(BLOCKS):
                    wait_apart(act, m_mm, 3 * n + b + 1)
                    act.activation(R.proj[:, m, t0:t0 + n_t], ps[:, slot, b, 0:n_t], ACT.Copy,
                                   scale=1 / WSCALE).then_inc(m_ev, 1)

            w_split(0, 0, 3)
            for t in range(TT):
                act.wait_ge(v_mm, t + 1)
                act.activation(R.v[:, t], psv[:, t % 2], ACT.Copy, scale=1 / WSCALE).then_inc(v_ev, 1)
            w_split(1, 1, 3)
            evacuate(0, 0, M_LOW)
            with act.Fori(0, 5) as i:
                w_split(2 + 2 * i, 0, i + 4)
                evacuate(1 + 2 * i, 1, 2 * i)
                w_split(3 + 2 * i, 1, i + 4)
                evacuate(2 + 2 * i, 0, 2 * i + 1)
            w_split(12, 0, 9)
            evacuate(11, 1, 10)
            evacuate(12, 0, 11)

        @block.vector
        def _(dve):
            def v_lo_part(k):
                dve.wait_ge(w_hi_ok, k + 1)
                dve.scalar_tensor_tensor(v_lo[:, 2 * k:2 * k + 2].rearrange("p a b -> p (a b)"), w_st[:, k % 2],
                                         WSCALE, v_hi[:, 2 * k:2 * k + 2].rearrange("p a b -> p (a b)"),
                                         ALU.mult, ALU.subtract).then_inc(w_lo_ok, 1)
            for k in range(KO):
                dve.wait_ge(x_hi_ok, k + 1)
                dve.tensor_tensor(x_lo[:, k], x_st[:, k % 2], x_hi[:, k], ALU.subtract).then_inc(x_lo_ok, 1)
                if k < 2:
                    v_lo_part(k)
            for k in range(2, NV):
                v_lo_part(k)

            def w_split(eng, n, slot, m, first):
                eng.wait_ge(w_hi_ok, n + NV + 1)
                eng.scalar_tensor_tensor(w_lo[:, slot].rearrange("p a b -> p (a b)"), w_st[:, slot], WSCALE,
                                         w_hi[:, slot].rearrange("p a b -> p (a b)"),
                                         ALU.mult, ALU.subtract).then_inc(w_lo_ok, 1)
            m_items(dve, w_split)

        @block.tensor
        def _(pe):
            pe.wait_ge(w_lo_ok, NV)
            for t in range(TT):
                if t >= 2:
                    pe.wait_ge(v_ev, t - 1)
                for k in range(KO):
                    if t == 0:
                        pe.wait_ge(x_lo_ok, k + 1)
                    last = hi_lo(pe, psv[:, t % 2], x_hi[:, k, t * P:(t + 1) * P], x_lo[:, k, t * P:(t + 1) * P],
                                 v_hi[:, k], v_lo[:, k], k == 0, k == KO - 1)
                last.then_inc(v_mm, 1)

            def tile(eng, n, slot, m, first):
                eng.wait_ge(w_lo_ok, n + NV + 1)
                for b, (t0, n_t) in enumerate(BLOCKS):
                    if not first:
                        eng.wait_ge(m_ev, 3 * n + b - 2)
                    for k in range(KO):
                        last = hi_lo(eng, ps[:, slot, b, 0:n_t], w_hi[:, slot, k], w_lo[:, slot, k],
                                     x_hi[:, k, t0:t0 + n_t], x_lo[:, k, t0:t0 + n_t], k == 0, k == KO - 1)
                    last.then_inc(m_mm, 1)
            m_items(pe, tile)


class Buffers:
    pass


def gated_attention(nc, A, R):
    with ExitStack() as c:
        sb = lambda n, s, d: c.enter_context(nc.sbuf_tensor(n, s, d))
        sem = lambda n: R.stack.enter_context(nc.semaphore(n))
        w_a2 = sb("a_w_a2", [2 * AB_ROW, HEADS * DK], f32)
        b_a = sb("a_b_a", [P, 4], f32)
        norm_g = sb("a_norm_g", [P, 1], f32)
        causal = sb("a_causal", [P, 2, P], f32)
        ident = sb("a_ident", [P, P], f32)
        ones = sb("a_ones", [P, P], f32)
        reset = sb("a_reset", [P, NT], f16)
        z = sb("a_z", [P, NT], f32)
        soft = sb("a_soft", [P, NT], f32)
        cum = sb("a_cum", [P, NT], f32)
        kk = sb("a_kk", [P, NT], f32)
        k_st = sb("a_k_st", [P, NT], f32)
        qq = sb("a_qq", [P, NT], f32)
        q_in = sb("a_q_in", [P, 2, NT], f32)
        k_nat = sb("a_k_nat", [P, TT, P], f32)
        probs = sb("a_probs", [P, 2, 2, TT, P], f32)
        state = sb("a_state", [P, 2, NCH, DV], f32)
        o_sb, o_sq, o_g, rms = z, soft, kk, qq
        ps_z = c.enter_context(nc.psum_tensor("a_ps_z", [P, 3, 512], f32))
        ps_x = c.enter_context(nc.psum_tensor("a_ps_x", [P, 3, 512], f32))
        ps_d = c.enter_context(nc.psum_tensor("a_ps_d", [P, 2, 4, DV], f32))
        flat_z = ps_z[:].rearrange("p a b -> p (a b)")
        flat_x = ps_x[:].rearrange("p a b -> p (a b)")

        consts, z_mm, z_ok, soft_ok, cum_ok, e_ok, gated = [sem("a_" + n) for n in
            "consts z_mm z_ok soft_ok cum_ok e_ok gated".split()]
        kt_mm, kt_ev, s_mm, s_ev, d_mm, st_ok, o_mm, o_ev = [sem("a_" + n) for n in
            "kt_mm kt_ev s_mm s_ev d_mm st_ok o_mm o_ev".split()]
        ms_mm, rms_ok, rec_ok, o_res, o_hi_ok, o_lo_ok, silu_ok, made, act_in, dve_in = [sem("a_" + n) for n in
            "ms_mm rms_ok rec_ok o_res o_hi_ok o_lo_ok silu_ok made act_in dve_in".split()]
        UNITS = [(pr, dr) for pr in range(PAIRS) for dr in range(2)]
        n0 = SEQS[0] // CHUNK
        ORDER = [[list(range(n0)), list(range(n0, NCH))], [list(range(n0 - 1, -1, -1)), list(range(NCH - 1, n0 - 1, -1))]]
        STEPS = [[(a, b) for seq in ORDER[dr] for a, b in zip(seq, seq[1:])] for dr in range(2)]
        NS = len(STEPS[0])
        FIRST = [[seq[0] for seq in ORDER[dr]] for dr in range(2)]
        LAST_C, MID_C = (CHUNK - 1, 0), (CHUNK // 2 - 1, CHUNK - CHUNK // 2)
        SLOT, BATCH = [], []
        for dr in range(2):
            SLOT.append([])
            BATCH.append([])
            used = [4, 4]
            for k, (a, _) in enumerate(STEPS[dr]):
                if used[a % 2] == 4:
                    used = [0, 0]
                    BATCH[dr].append(k)
                SLOT[dr].append((len(BATCH[dr]) - 1, a % 2, used[a % 2]))
                used[a % 2] += 1
            BATCH[dr].append(NS)

        def delta(dr, k):
            batch, bank, slot = SLOT[dr][k]
            if batch % 2:
                return ps_z[:, bank, slot * DV:(slot + 1) * DV]
            return ps_d[:, bank, slot]

        def by_chunk(ap, at):
            v = ap.rearrange("p (n c) -> p n c", c=CHUNK)
            return v, v[:, :, at:at + 1].to_broadcast([P, NCH, CHUNK])

        block = c.enter_context(nc.Block())

        @block.sync
        def _(sp):
            for dst, src in ((w_a2, "w_a2"), (b_a, "b_a"), (norm_g, "norm_g"), (causal, "causal"), (ident, "ident")):
                sp.dma_start(dst[:], A[src]).then_inc(consts, 16)

        @block.scalar
        def _(act):
            r_all = R.proj[:, M_R:M_R + 4].rearrange("p a b -> p (a b)")
            act.activation(r_all, r_all, ACT.Silu).then_inc(silu_ok, 1)
            act.wait_ge(consts, 16 * 5)

            def gate(u):
                act.wait_ge(z_mm, u + 1)
                if u:
                    act.wait_ge(cum_ok, u)
                if u == 2:
                    act.wait_ge(o_res, 2)
                act.activation(z[:], flat_z[:, 0:NT], ACT.Identity, bias=b_a[:, u:u + 1]).then_inc(z_ok, 1)
                act.wait_ge(z_ok, u + 1)
                act.activation(soft[:], z[:], ACT.Abs).then_inc(act_in, 1)
                act.wait_ge(act_in, 2 * u + 1)
                act.activation(soft[:], soft[:], ACT.Exp, scale=-1.0).then_inc(act_in, 1)
                act.wait_ge(act_in, 2 * u + 2)
                act.activation(soft[:], soft[:], ACT.Ln, bias=1.0).then_inc(soft_ok, 1)
                act.wait_ge(cum_ok, u + 1)
                act.activation(qq[:], kk[:], ACT.Exp, scale=1 / 16)
                act.activation(kk[:], kk[:], ACT.Exp, scale=-1 / 16)
                act.activation(cum[:], cum[:], ACT.Exp, scale=1 / 16)
                act.activation(k_st[:], k_st[:], ACT.Exp, scale=1 / 16).then_inc(e_ok, 1)

            def keys(u):
                act.wait_ge(kt_mm, u + 1)
                if u:
                    act.wait_ge(d_mm, 2 * NS * u)
                act.activation(k_nat[:].rearrange("p a b -> p (a b)"), flat_x[:, 0:NT], ACT.Copy).then_inc(kt_ev, 1)

            def out(pr, h):
                n = 2 * pr + h
                act.wait_ge(o_mm, n + 1)
                if h:
                    act.wait_ge(o_res, n)
                act.activation(o_sb[:], flat_x[:, 0:NT], ACT.Copy).then_inc(o_ev, 1)
                act.wait_ge(o_ev, 2 * n + 1)
                act.activation(o_sq[:], o_sb[:], ACT.Square, scale=DV ** -0.5).then_inc(o_ev, 1)
                act.wait_ge(rms_ok, n + 1)
                act.activation(rms[:], rms[:], ACT.Sqrt).then_inc(rec_ok, 1)
                act.wait_ge(o_res, n + 1)
                act.activation(R.o_hi[:, n], k_nat_f, ACT.Copy).then_inc(o_hi_ok, 1)

            k_nat_f = k_nat[:].rearrange("p a b -> p (a b)")
            for pr in range(PAIRS):
                for dr in range(2):
                    gate(2 * pr + dr)
                    keys(2 * pr + dr)
                for h in range(2):
                    out(pr, h)

        @block.vector
        def _(dve):
            dve.memset(reset[:], 1.0)
            dve.memset(probs[:].rearrange("p a b c d -> p (a b c d)"), 0.0)
            for dr in range(2):
                for n in FIRST[dr]:
                    dve.memset(state[:, dr, n], 0.0)
            dve.memset(ones[:], 1.0).then_inc(made, 1)
            dve.wait_ge(made, 1)
            dve.memset(reset[:].rearrange("p (n c) -> p n c", c=CHUNK)[:, :, 0:1], 0.0).then_inc(made, 1)
            dve.wait_ge(made, 2)
            chain = [0]

            def link(ins):
                chain[0] += 1
                ins.then_inc(dve_in, 1)
                dve.wait_ge(dve_in, chain[0])

            def unit(u, pr, dr):
                dve.wait_ge(soft_ok, u + 1)
                link(dve.scalar_tensor_tensor(z[:], z[:], 0.0, soft[:], ALU.min, ALU.subtract))
                link(dve.tensor_tensor_scan(cum[:], reset[:], z[:], 0.0, ALU.mult, ALU.add))
                if dr:
                    link(dve.tensor_tensor(z[:], z[:], cum[:], ALU.subtract))
                    v, last = by_chunk(cum[:], CHUNK - 1)
                    link(dve.tensor_tensor(z[:].rearrange("p (n c) -> p n c", c=CHUNK),
                                           z[:].rearrange("p (n c) -> p n c", c=CHUNK), last, ALU.add))
                    link(dve.tensor_copy(cum[:], z[:]))
                v, mid = by_chunk(cum[:], MID_C[dr])
                v, last = by_chunk(cum[:], LAST_C[dr])
                if u:
                    dve.wait_ge(s_mm, 2 * u)
                    dve.wait_ge(kt_mm, u)
                dve.tensor_tensor(kk[:].rearrange("p (n c) -> p n c", c=CHUNK), v, mid, ALU.subtract)
                dve.tensor_tensor(k_st[:].rearrange("p (n c) -> p n c", c=CHUNK), last, v,
                                  ALU.subtract).then_inc(cum_ok, 1)
                dve.wait_ge(e_ok, u + 1)
                if u == 2:
                    dve.wait_ge(o_mm, 2)
                q, k = R.proj[:, M_Q + pr], R.proj[:, M_K + pr]
                dve.scalar_tensor_tensor(qq[:], q, DK ** -0.5, qq[:], ALU.mult, ALU.mult)
                dve.tensor_tensor(kk[:], k, kk[:], ALU.mult)
                dve.scalar_tensor_tensor(q_in[:, dr], q, DK ** -0.5, cum[:], ALU.mult, ALU.mult)
                dve.tensor_tensor(k_st[:], k, k_st[:], ALU.mult).then_inc(gated, 1)
                for h in range(2):
                    dve.wait_ge(s_mm, 2 * u + h + 1)
                    if u >= 2:
                        dve.wait_ge(o_mm, 2)
                    dve.copy_predicated(probs[:, dr, h], causal[:, dr:dr + 1].bitcast(u32).to_broadcast([P, TT, P]),
                                        flat_x[:, 0:NT].rearrange("p (n c) -> p n c", c=P)).then_inc(s_ev, 1)
                for k, (a, b) in enumerate(STEPS[dr]):
                    if k in BATCH[dr]:
                        dve.wait_ge(d_mm, 2 * (NS * u + BATCH[dr][SLOT[dr][k][0] + 1]))
                    if k:
                        dve.wait_ge(st_ok, NS * u + k)
                    at = a * CHUNK + LAST_C[dr]
                    dve.scalar_tensor_tensor(state[:, dr, b], state[:, dr, a], cum[:, at:at + 1],
                                             delta(dr, k), ALU.mult, ALU.add).then_inc(st_ok, 1)

            def out(n):
                dve.wait_ge(ms_mm, n + 1)
                link(dve.tensor_scalar(rms[:], flat_z[:, 0:NT], RMS_EPS, None, ALU.add))
                dve.reciprocal(rms[:], rms[:]).then_inc(rms_ok, 1)
                link(dve.tensor_scalar(o_g[:], o_sb[:], norm_g[:, 0:1], None, ALU.mult))
                link(dve.tensor_tensor(o_g[:], o_g[:], R.proj[:, M_R + n], ALU.mult))
                dve.wait_ge(rec_ok, n + 1)
                if n % 2 == 0:
                    dve.wait_ge(d_mm, 2 * NS * (n + 2))
                dve.tensor_tensor(k_nat_f, o_g[:], rms[:], ALU.mult).then_inc(o_res, 1)
                dve.wait_ge(o_hi_ok, n + 1)
                dve.tensor_tensor(R.o_lo[:, n], k_nat_f, R.o_hi[:, n], ALU.subtract).then_inc(o_lo_ok, 1)
                dve.wait_ge(o_lo_ok, n + 1)

            k_nat_f = k_nat[:].rearrange("p a b -> p (a b)")
            dve.wait_ge(silu_ok, 1)
            dve.wait_ge(consts, 16 * 5)
            for pr in range(PAIRS):
                for dr in range(2):
                    unit(2 * pr + dr, pr, dr)
                for h in range(2):
                    out(2 * pr + h)

        @block.tensor
        def _(pe):
            pe.wait_ge(consts, 16 * 5)
            pe.wait_ge(made, 2)

            def gates(u):
                pr, dr = divmod(u, 2)
                if u:
                    pe.wait_ge(st_ok, NS * u)
                if u == 2:
                    pe.wait_ge(rms_ok, 2)
                r0 = AB_ROW * dr
                for b, (t0, n_t) in enumerate(BLOCKS):
                    last = pe.matmul(ps_z[:, b, 0:n_t], w_a2[r0:r0 + RANK, pr * P:(pr + 1) * P],
                                     R.proj[r0:r0 + RANK, M_LOW, t0:t0 + n_t], start=True, stop=True)
                last.then_inc(z_mm, 1)

            def unit(u, pr, dr):
                pe.wait_ge(gated, u + 1)
                if u:
                    pe.wait_ge(s_ev, 2 * u)
                if u == 2:
                    pe.wait_ge(o_ev, 4)
                for n in range(TT):
                    last = pe.transpose(flat_x[:, n * P:(n + 1) * P], k_st[:, n * P:(n + 1) * P], ident[:])
                last.then_inc(kt_mm, 1)
                for h in range(2):
                    rows = slice(DK * h, DK * (h + 1))
                    if h == 0:
                        pe.wait_ge(kt_ev, u + 1)
                    else:
                        pe.wait_ge(s_ev, 2 * u + 1)
                    for n in range(TT):
                        t = slice(n * P, (n + 1) * P)
                        last = pe.matmul(flat_x[:, t], kk[rows, t], qq[rows, t], start=True, stop=True)
                    last.then_inc(s_mm, 1)
                for k, (a, _) in enumerate(STEPS[dr]):
                    batch = SLOT[dr][k][0]
                    if k in BATCH[dr] and batch >= 2:
                        pe.wait_ge(st_ok, NS * u + BATCH[dr][batch - 1])
                    elif k == 0 and u:
                        pe.wait_ge(st_ok, NS * u)
                    for h in range(2):
                        rows = slice(CHUNK * (a % 2), CHUNK * (a % 2 + 1))
                        pe.matmul(delta(dr, k)[DK * h:DK * (h + 1)], k_nat[rows, a // 2, DK * h:DK * (h + 1)],
                                  R.v[rows, a // 2, (2 * pr + h) * DV:(2 * pr + h + 1) * DV],
                                  start=True, stop=True).then_inc(d_mm, 1)

            def out(pr, h):
                n_h = 2 * pr + h
                pe.wait_ge(st_ok, NS * (2 * pr + 2))
                pe.wait_ge(s_ev, 2 * (2 * pr + 2))
                if h:
                    pe.wait_ge(o_ev, 2 * n_h - 1)
                rows = slice(DK * h, DK * (h + 1))
                for n in range(TT):
                    t = slice(n * P, (n + 1) * P)
                    v = R.v[:, n, n_h * DV:(n_h + 1) * DV]
                    pe.matmul(flat_x[:, t], v, probs[:, 0, h, n], start=True, stop=False)
                    more = [(dr, ch) for ch in (2 * n, 2 * n + 1) for dr in range(2) if ch not in FIRST[dr]]
                    last = pe.matmul(flat_x[:, t], v, probs[:, 1, h, n], start=False, stop=not more)
                    for m, (dr, ch) in enumerate(more):
                        tc = slice(ch * CHUNK, (ch + 1) * CHUNK)
                        last = pe.matmul(flat_x[:, tc], state[rows, dr, ch], q_in[rows, dr, tc],
                                         start=False, stop=m == len(more) - 1)
                last.then_inc(o_mm, 1)

            def mean_square(n_h):
                pe.wait_ge(o_ev, 2 * n_h + 2)
                if n_h % 2:
                    pe.wait_ge(rms_ok, n_h)
                for b, (t0, n_t) in enumerate(BLOCKS):
                    last = pe.matmul(ps_z[:, b, 0:n_t], ones[:], o_sq[:, t0:t0 + n_t], start=True, stop=True)
                last.then_inc(ms_mm, 1)

            for pr in range(PAIRS):
                for dr in range(2):
                    gates(2 * pr + dr)
                    unit(2 * pr + dr, pr, dr)
                for h in range(2):
                    out(pr, h)
                    mean_square(2 * pr + h)


def fourier(nc, A, R):
    with ExitStack() as c:
        sb = lambda n, s, d: c.enter_context(nc.sbuf_tensor(n, s, d))
        sem = lambda n: R.stack.enter_context(nc.semaphore(n))
        KT = SEQS[0] // P
        f_hi, f_lo = sb("f_f_hi", [P, NT], f16), sb("f_f_lo", [P, NT], f16)
        dft_c = sb("f_dft_c", [P, 2, 2 * GDIM], f16)
        dft_t = sb("f_dft_t", [P, 2, 2, KT, SEQS[0]], f16)
        dft_s = sb("f_dft_s", [P, 2, 2, SEQS[1] // P, SEQS[1]], f16)
        ab = sb("f_ab", [P, 2, 2 * GDIM], f32)
        ab_hi, ab_lo = sb("f_ab_hi", [P, 2, TT, 2 * GDIM], f16), sb("f_ab_lo", [P, 2, TT, 2 * GDIM], f16)
        out = sb("f_out", [P, 2, 512], f32)
        ps_c = c.enter_context(nc.psum_tensor("f_ps_c", [P, 4, 512], f32))
        ps_t = c.enter_context(nc.psum_tensor("f_ps_t", [P, 4, 512], f32))
        tables, f_hi_ok, f_lo_ok, c_mm, c_ev, c_hi, c_lo, t_mm, t_ev, t_hi, t_lo = [sem("f_" + n) for n in
            "tables f_hi_ok f_lo_ok c_mm c_ev c_hi c_lo t_mm t_ev t_hi t_lo".split()]
        time_in = sem("f_time_in")
        BANKS = [(0, 512, 0, KT, dft_t, 0), (512, 512, 0, KT, dft_t, 512), (SEQS[0], SEQS[1], KT, SEQS[1] // P, dft_s, 0)]

        def in_order(channels, time):
            channels(0)
            for g in range(GROUPS):
                if g + 1 < GROUPS:
                    channels(g + 1)
                time(g)
        block = c.enter_context(nc.Block())

        @block.sync
        def _(sp):
            sp.dma_start(dft_c[:], A["dft_c"]).then_inc(tables, 16)
            sp.dma_start(dft_t[:], A["dft_t"]).then_inc(time_in, 16)
            sp.dma_start(dft_s[:], A["dft_s"]).then_inc(time_in, 16)

        @block.scalar
        def _(act):
            def channels(g):
                if g:
                    act.wait_ge(c_mm, TT * g)
                if g >= 2:
                    act.wait_ge(t_mm, NB * (g - 1))
                act.activation(f_hi[:], R.proj[:, M_F + g], ACT.Copy).then_inc(f_hi_ok, 1)
                for t in range(TT):
                    n = TT * g + t
                    act.wait_ge(c_mm, n + 1)
                    if n >= 2:
                        act.wait_ge(c_lo, n - 1)
                    act.activation(ab[:, n % 2], ps_c[:, n % 4, 0:2 * GDIM], ACT.Copy,
                                   scale=GDIM ** -0.5 / WSCALE).then_inc(c_ev, 1)
                    act.wait_ge(c_ev, n + 1)
                    act.activation(ab_hi[:, g % 2, t], ab[:, n % 2], ACT.Copy).then_inc(c_hi, 1)

            def time(g):
                for b, (t0, n_t, *_) in enumerate(BANKS):
                    n = NB * g + b
                    act.wait_ge(t_mm, n + 1)
                    if n >= 2:
                        act.wait_ge(t_lo, n - 1)
                    act.activation(out[:, n % 2, 0:n_t], ps_t[:, n % 4, 0:n_t], ACT.Copy,
                                   scale=(SEQS[0] if t0 < SEQS[0] else SEQS[1]) ** -0.5 / WSCALE).then_inc(t_ev, 1)
                    act.wait_ge(t_ev, n + 1)
                    act.activation(R.f_hi[:, g, t0:t0 + n_t], out[:, n % 2, 0:n_t], ACT.Copy).then_inc(t_hi, 1)
            in_order(channels, time)

        @block.vector
        def _(dve):
            def channels(g):
                dve.wait_ge(f_hi_ok, g + 1)
                dve.tensor_tensor(f_lo[:], R.proj[:, M_F + g], f_hi[:], ALU.subtract).then_inc(f_lo_ok, 1)
                for t in range(TT):
                    n = TT * g + t
                    dve.wait_ge(c_hi, n + 1)
                    dve.tensor_tensor(ab_lo[:, g % 2, t], ab[:, n % 2], ab_hi[:, g % 2, t], ALU.subtract).then_inc(c_lo, 1)

            def time(g):
                for b, (t0, n_t, *_) in enumerate(BANKS):
                    n = NB * g + b
                    dve.wait_ge(t_hi, n + 1)
                    dve.tensor_tensor(R.f_lo[:, g, t0:t0 + n_t], out[:, n % 2, 0:n_t], R.f_hi[:, g, t0:t0 + n_t],
                                      ALU.subtract).then_inc(t_lo, 1)
            in_order(channels, time)

        @block.tensor
        def _(pe):
            pe.wait_ge(tables, 16)
            def channels(g):
                pe.wait_ge(f_lo_ok, g + 1)
                for t in range(TT):
                    n = TT * g + t
                    if n >= 4:
                        pe.wait_ge(c_ev, n - 3)
                    cols = slice(t * P, (t + 1) * P)
                    hi_lo(pe, ps_c[:, n % 4, 0:2 * GDIM], f_hi[:, cols], f_lo[:, cols], dft_c[:, 0], dft_c[:, 1],
                          True, True).then_inc(c_mm, 1)

            def time(g):
                pe.wait_ge(c_lo, TT * (g + 1))
                pe.wait_ge(time_in, 32)
                for b, (t0, n_t, k0, n_k, table, col) in enumerate(BANKS):
                    n = NB * g + b
                    if n >= 4:
                        pe.wait_ge(t_ev, n - 3)
                    for k in range(n_k):
                        for s in range(2):
                            ch = slice(s * GDIM, (s + 1) * GDIM)
                            last = hi_lo(pe, ps_t[:, n % 4, 0:n_t], ab_hi[:, g % 2, k0 + k, ch],
                                         ab_lo[:, g % 2, k0 + k, ch], table[:, s, 0, k, col:col + n_t],
                                         table[:, s, 1, k, col:col + n_t], k == 0 and s == 0, k == n_k - 1 and s == 1)
                    last.then_inc(t_mm, 1)
            in_order(channels, time)


def merge(nc, A, R):
    with ExitStack() as c:
        sb = lambda n, s, d: c.enter_context(nc.sbuf_tensor(n, s, d))
        sem = lambda n: R.stack.enter_context(nc.semaphore(n))
        x_hi, x_lo = sb("m_x_hi", [P, KO, NT], f16), sb("m_x_lo", [P, KO, NT], f16)
        KW = 2 * KO + 2 * HEADS
        w_st = sb("m_w_st", [P, 2, KW * P], f32)
        w_hi, w_lo = sb("m_w_hi", [P, 2, KW * P], f16), sb("m_w_lo", [P, 2, KW * P], f16)
        b_mg = sb("m_b_mg", [P, 2, KO], f32)
        s1, s2 = sb("m_s1", [P, 2, 512], f32), sb("m_s2", [P, 2, 512], f32)
        t1, t2, mg = sb("m_t1", [P, 512], f32), sb("m_t2", [P, 512], f32), sb("m_mg", [P, 2, 512], f32)
        ps = c.enter_context(nc.psum_tensor("m_ps", [P, 2, 4, 512], f32))
        x_in, bias_in = sem("m_x_in"), sem("m_bias_in")
        w_in = [sem("m_w_in0"), sem("m_w_in1")]
        w_hi_ok, w_lo_ok, mm, sig, prod, mg_ok, mg_hi, mg_lo = [sem("m_" + n) for n in
            "w_hi_ok w_lo_ok mm sig prod mg_ok mg_hi mg_lo".split()]
        block = c.enter_context(nc.Block())

        @block.sync
        def _(sp):
            sp.dma_start(w_st[:, 0], A["w_merge"][0]).then_inc(w_in[0], 16)
            sp.dma_start(x_hi[:], R.x_hi_dram).then_inc(x_in, 16)
            sp.dma_start(x_lo[:], R.x_lo_dram).then_inc(x_in, 16)
            sp.dma_start(b_mg[:], A["b_mg"]).then_inc(bias_in, 16)
            sp.dma_start(w_st[:, 1], A["w_merge"][1]).then_inc(w_in[1], 16)
            with sp.Fori(1, KO // 2) as i:
                for q in range(2):
                    sp.wait_ge(w_lo_ok, 2 * i + q - 1)
                    sp.dma_start(w_st[:, q], A["w_merge"][2 * i + q]).then_inc(w_in[q], 16)

        def split_hi(act, m, q, nth):
            act.wait_ge(w_in[q], nth)
            if not isinstance(m, int) or m >= 2:
                act.wait_ge(mm, NB * (m - 1))
            act.activation(w_hi[:, q], w_st[:, q], ACT.Copy, scale=WSCALE).then_inc(w_hi_ok, 1)

        @block.scalar
        def _(act):
            def steps(m, q):
                for b, (t0, n_t) in enumerate(BLOCKS):
                    n, s = NB * m + b, (NB * q + b) % 2
                    act.wait_ge(mm, n + 1)
                    if not (isinstance(n, int) and n < 2):
                        wait_apart(act, mg_ok, n - 1)
                    act.activation(s1[:, s, 0:n_t], ps[:, s, 0, 0:n_t], ACT.Sigmoid, scale=1 / WSCALE,
                                   bias=b_mg[:, 0, m:m + 1] if isinstance(m, int) else b_mg[:, 0, bass.ds(m, 1)])
                    act.activation(s2[:, s, 0:n_t], ps[:, s, 1, 0:n_t], ACT.Sigmoid, scale=1 / WSCALE,
                                   bias=b_mg[:, 1, m:m + 1] if isinstance(m, int) else b_mg[:, 1, bass.ds(m, 1)]
                                   ).then_inc(sig, 1)
                    wait_apart(act, mg_ok, n + 1)
                    act.activation(R.m_hi[:, m, t0:t0 + n_t], mg[:, s, 0:n_t], ACT.Copy).then_inc(mg_hi, 1)
            act.wait_ge(bias_in, 16)
            split_hi(act, 0, 0, 16)
            split_hi(act, 1, 1, 16)
            steps(0, 0)
            with act.Fori(1, KO // 2) as i:
                split_hi(act, 2 * i, 0, 16 * i + 16)
                steps(2 * i - 1, 1)
                split_hi(act, 2 * i + 1, 1, 16 * i + 16)
                steps(2 * i, 0)
            steps(KO - 1, 1)

        @block.vector
        def _(dve):
            def split_lo(m, q):
                dve.wait_ge(w_hi_ok, m + 1)
                dve.scalar_tensor_tensor(w_lo[:, q], w_st[:, q], WSCALE, w_hi[:, q], ALU.mult,
                                         ALU.subtract).then_inc(w_lo_ok, 1)

            def steps(m, q):
                for b, (t0, n_t) in enumerate(BLOCKS):
                    n, s = NB * m + b, (NB * q + b) % 2
                    dve.wait_ge(sig, n + 1)
                    dve.scalar_tensor_tensor(t1[:, 0:n_t], ps[:, s, 2, 0:n_t], 1 / WSCALE, s1[:, s, 0:n_t],
                                             ALU.mult, ALU.mult)
                    dve.scalar_tensor_tensor(t2[:, 0:n_t], ps[:, s, 3, 0:n_t], 1 / WSCALE, s2[:, s, 0:n_t],
                                             ALU.mult, ALU.mult).then_inc(prod, 1)
                    dve.wait_ge(prod, n + 1)
                    dve.tensor_tensor(mg[:, s, 0:n_t], t1[:, 0:n_t], t2[:, 0:n_t], ALU.add).then_inc(mg_ok, 1)
                    dve.wait_ge(mg_hi, n + 1)
                    dve.tensor_tensor(R.m_lo[:, m, t0:t0 + n_t], mg[:, s, 0:n_t], R.m_hi[:, m, t0:t0 + n_t],
                                      ALU.subtract).then_inc(mg_lo, 1)
            split_lo(0, 0)
            split_lo(1, 1)
            steps(0, 0)
            with dve.Fori(1, KO // 2) as i:
                split_lo(2 * i, 0)
                steps(2 * i - 1, 1)
                split_lo(2 * i + 1, 1)
                steps(2 * i, 0)
            steps(KO - 1, 1)

        @block.tensor
        def _(pe):
            def tile(m, q, peeled):
                pe.wait_ge(w_lo_ok, m + 1)
                for b, (t0, n_t) in enumerate(BLOCKS):
                    n, s = NB * m + b, (NB * q + b) % 2
                    if not (isinstance(n, int) and n < 2):
                        pe.wait_ge(mg_ok, n - 1)
                    t = slice(t0, t0 + n_t)
                    at = 0
                    for o, (hi, lo, n_k) in enumerate(((x_hi, x_lo, KO), (x_hi, x_lo, KO),
                                                       (R.o_hi, R.o_lo, HEADS), (R.f_hi, R.f_lo, GROUPS))):
                        for k in range(n_k):
                            w = slice(at * P, (at + 1) * P)
                            last = hi_lo(pe, ps[:, s, o, 0:n_t], w_hi[:, q, w], w_lo[:, q, w], hi[:, k, t], lo[:, k, t],
                                         k == 0, k == n_k - 1)
                            at += 1
                    last.then_inc(mm, 1)
            pe.wait_ge(x_in, 32)
            tile(0, 0, True)
            tile(1, 1, True)
            with pe.Fori(1, KO // 2) as i:
                tile(2 * i, 0, False)
                tile(2 * i + 1, 1, False)


def layer_norm_steps(dve, y, stats, mv, gain, shift, link, rms_ready, rms_taken, n):
    for half in range(2):
        last = dve.bn_stats(stats[:, half], y[:, half * 512:(half + 1) * 512])
    link(last)
    link(dve.bn_aggr(mv[:, 0:2], stats[:].rearrange("p a b -> p (a b)")))
    dve.tensor_scalar(mv[:, 2:3], mv[:, 1:2], LN_EPS, None, ALU.add).then_inc(rms_ready, 1)
    dve.wait_ge(rms_taken, n + 1)
    link(dve.reciprocal(mv[:, 3:4], mv[:, 2:3]))
    link(dve.tensor_scalar(y, y, mv[:, 0:1], mv[:, 3:4], ALU.subtract, ALU.mult))
    link(dve.tensor_tensor(y, y, gain, ALU.mult))
    return dve.tensor_tensor(y, y, shift, ALU.add)


def linker(dve, sem):
    chain = [0]

    def link(ins):
        chain[0] += 1
        ins.then_inc(sem, 1)
        dve.wait_ge(sem, chain[0])
    return link


def mix_norm(nc, A, R):
    with ExitStack() as c:
        sb = lambda n, s, d: c.enter_context(nc.sbuf_tensor(n, s, d))
        sem = lambda n: R.stack.enter_context(nc.semaphore(n))
        w_st = sb("o_w_st", [P, 2, D], f32)
        w_hi, w_lo = sb("o_w_hi", [P, KO, D], f16), sb("o_w_lo", [P, KO, D], f16)
        x = sb("o_x", [P, 2, D], f32)
        y = sb("o_y", [P, 2, D], f32)
        gain, shift = sb("o_gain", [P, D], f32), sb("o_shift", [P, D], f32)
        ident = sb("o_ident", [P, P], f32)
        stats, mv = sb("o_stats", [P, 2, 6], f32), sb("o_mv", [P, 4], f32)
        ps = c.enter_context(nc.psum_tensor("o_ps", [P, 2, D], f32))
        ps_t = c.enter_context(nc.psum_tensor("o_ps_t", [P, 2, KO, P], f32))
        w_in = [sem("o_w_in0"), sem("o_w_in1")]
        x_in = [sem("o_x_in0"), sem("o_x_in1")]
        consts, w_hi_ok, w_lo_ok, mm, ax_ok, y_ok, v_ok, sq_ok, h_ok, t_mm, acc_ok, hi_ok, lo_ok, dve_in = [
            sem("o_" + n) for n in "consts w_hi_ok w_lo_ok mm ax_ok y_ok v_ok sq_ok h_ok t_mm acc_ok hi_ok lo_ok dve_in".split()]
        block = c.enter_context(nc.Block())

        @block.sync
        def _(sp):
            for k in range(KO):
                if k >= 2:
                    sp.wait_ge(w_lo_ok, k - 1)
                sp.dma_start(w_st[:, k % 2], A["w_o"][k]).then_inc(w_in[k % 2], 16)
                if k == 1:
                    sp.dma_start(gain[:], A["ln1_g"].to_broadcast([P, D])).then_inc(consts, 16)
                    sp.dma_start(shift[:], A["ln1_b"].to_broadcast([P, D])).then_inc(consts, 16)
                    sp.dma_start(ident[:], A["ident"]).then_inc(consts, 16)
                    for t in range(2):
                        sp.dma_start(x[:, t], A["x"][t]).then_inc(x_in[t], 16)
            for t in range(2, TT):
                sp.wait_ge(y_ok, t - 1)
                sp.dma_start(x[:, t % 2], A["x"][t]).then_inc(x_in[t % 2], 16)

        @block.scalar
        def _(act):
            for k in range(KO):
                act.wait_ge(w_in[k % 2], 16 * (k // 2 + 1))
                act.activation(w_hi[:, k], w_st[:, k % 2], ACT.Copy, scale=WSCALE).then_inc(w_hi_ok, 1)

            def scaled_x(t):
                act.wait_ge(x_in[t % 2], 16 * (t // 2 + 1))
                act.activation(x[:, t % 2], x[:, t % 2], ACT.Copy, scale=ALPHA).then_inc(ax_ok, 1)
            scaled_x(0)
            for t in range(TT):
                act.wait_ge(v_ok, t + 1)
                act.activation(mv[:, 2:3], mv[:, 2:3], ACT.Sqrt).then_inc(sq_ok, 1)
                if t + 1 < TT:
                    scaled_x(t + 1)
                act.wait_ge(h_ok, t + 1)
                if t >= DT:
                    act.activation(R.h_nat[:, t - DT], y[:, t % 2], ACT.Copy)
                act.activation(R.acc[:, t], y[:, t % 2], ACT.Copy, scale=ALPHA).then_inc(acc_ok, 1)
                act.wait_ge(t_mm, t + 1)
                act.activation(R.h_hi[:, :, t * P:(t + 1) * P], ps_t[:, t % 2], ACT.Copy).then_inc(hi_ok, 1)

        @block.vector
        def _(dve):
            for k in range(KO):
                dve.wait_ge(w_hi_ok, k + 1)
                dve.scalar_tensor_tensor(w_lo[:, k], w_st[:, k % 2], WSCALE, w_hi[:, k], ALU.mult,
                                         ALU.subtract).then_inc(w_lo_ok, 1)
            link = linker(dve, dve_in)
            dve.wait_ge(consts, 48)

            def low_part(t):
                dve.wait_ge(hi_ok, t + 1)
                dve.tensor_tensor(R.h_lo[:, :, t * P:(t + 1) * P], ps_t[:, t % 2], R.h_hi[:, :, t * P:(t + 1) * P],
                                  ALU.subtract).then_inc(lo_ok, 1)
            for t in range(TT):
                dve.wait_ge(mm, t + 1)
                dve.wait_ge(ax_ok, t + 1)
                if t >= 2:
                    dve.wait_ge(acc_ok, t - 1)
                    dve.wait_ge(t_mm, t - 1)
                dve.scalar_tensor_tensor(y[:, t % 2], ps[:, t % 2], 1 / WSCALE, x[:, t % 2], ALU.mult,
                                         ALU.add).then_inc(y_ok, 1)
                dve.wait_ge(y_ok, t + 1)
                layer_norm_steps(dve, y[:, t % 2], stats, mv, gain[:], shift[:], link, v_ok, sq_ok, t).then_inc(h_ok, 1)
                if t:
                    low_part(t - 1)
            low_part(TT - 1)

        @block.tensor
        def _(pe):
            pe.wait_ge(consts, 48)
            pe.wait_ge(w_lo_ok, KO)

            def transposes(t):
                pe.wait_ge(h_ok, t + 1)
                if t >= 2:
                    pe.wait_ge(lo_ok, t - 1)
                for k in range(KO):
                    last = pe.transpose(ps_t[:, t % 2, k], y[:, t % 2, k * P:(k + 1) * P], ident[:])
                last.then_inc(t_mm, 1)
            for t in range(TT):
                if t >= 2:
                    pe.wait_ge(y_ok, t - 1)
                for k in range(KO):
                    lhs = R.m_hi[:, k, t * P:(t + 1) * P], R.m_lo[:, k, t * P:(t + 1) * P]
                    for half in range(2):
                        n = slice(half * 512, (half + 1) * 512)
                        last = hi_lo(pe, ps[:, t % 2, n], *lhs, w_hi[:, k, n], w_lo[:, k, n], k == 0, k == KO - 1)
                last.then_inc(mm, 1)
                if t:
                    transposes(t - 1)
            transposes(TT - 1)


def embed(nc, A, R):
    with ExitStack() as c:
        sb = lambda n, s, d: c.enter_context(nc.sbuf_tensor(n, s, d))
        sem = lambda n: R.stack.enter_context(nc.semaphore(n))
        KP = PLE // P
        w_st = sb("e_w_st", [P, 2, D], f32)
        w_hi, w_lo = sb("e_w_hi", [P, KO + KP, D], f16), sb("e_w_lo", [P, KO + KP, D], f16)
        p_st = sb("e_p_st", [P, KP, NT], f32)
        p_hi, p_lo = sb("e_p_hi", [P, KP, NT], f16), sb("e_p_lo", [P, KP, NT], f16)
        s = sb("e_s", [P, 2, D], f32)
        ps_g = c.enter_context(nc.psum_tensor("e_ps_g", [P, 2, D], f32))
        ps_p = c.enter_context(nc.psum_tensor("e_ps_p", [P, 2, D], f32))
        w_in = [sem("e_w_in0"), sem("e_w_in1")]
        p_in, w_hi_ok, w_lo_ok, p_hi_ok, p_lo_ok, mm, sig, prod, added = [sem("e_" + n) for n in
            "p_in w_hi_ok w_lo_ok p_hi_ok p_lo_ok mm sig prod added".split()]
        block = c.enter_context(nc.Block())

        @block.sync
        def _(sp):
            for k in range(KO + KP):
                if k >= 2:
                    sp.wait_ge(w_lo_ok, k - 1)
                sp.dma_start(w_st[:, k % 2], A["w_ple"][k]).then_inc(w_in[k % 2], 16)
                if k == 1:
                    sp.dma_start(p_st[:], A["p_t"]).then_inc(p_in, 16)

        @block.scalar
        def _(act):
            for k in range(KO + KP):
                act.wait_ge(w_in[k % 2], 16 * (k // 2 + 1))
                act.activation(w_hi[:, k], w_st[:, k % 2], ACT.Copy, scale=WSCALE).then_inc(w_hi_ok, 1)
            act.wait_ge(p_in, 16)
            act.activation(p_hi[:], p_st[:], ACT.Copy).then_inc(p_hi_ok, 1)
            for t in range(TT):
                act.wait_ge(mm, t + 1)
                if t >= 2:
                    act.wait_ge(added, t - 1)
                act.activation(s[:, t % 2], ps_g[:, t % 2], ACT.Sigmoid, scale=1 / WSCALE).then_inc(sig, 1)

        @block.vector
        def _(dve):
            for k in range(KO + KP):
                dve.wait_ge(w_hi_ok, k + 1)
                dve.scalar_tensor_tensor(w_lo[:, k], w_st[:, k % 2], WSCALE, w_hi[:, k], ALU.mult,
                                         ALU.subtract).then_inc(w_lo_ok, 1)
            dve.wait_ge(p_hi_ok, 1)
            dve.tensor_tensor(p_lo[:], p_st[:], p_hi[:], ALU.subtract).then_inc(p_lo_ok, 1)
            for t in range(TT):
                dve.wait_ge(sig, t + 1)
                dve.scalar_tensor_tensor(s[:, t % 2], ps_p[:, t % 2], 1 / WSCALE, s[:, t % 2], ALU.mult,
                                         ALU.mult).then_inc(prod, 1)
                dve.wait_ge(prod, t + 1)
                dve.tensor_tensor(R.acc[:, t], R.acc[:, t], s[:, t % 2], ALU.add).then_inc(added, 1)

        @block.tensor
        def _(pe):
            pe.wait_ge(w_lo_ok, KO + KP)
            pe.wait_ge(p_lo_ok, 1)
            for t in range(TT):
                if t >= 2:
                    pe.wait_ge(added, t - 1)
                for (out, hi, lo, k0, n_k) in ((ps_g, R.h_hi, R.h_lo, 0, KO), (ps_p, p_hi, p_lo, KO, KP)):
                    for k in range(n_k):
                        lhs = hi[:, k, t * P:(t + 1) * P], lo[:, k, t * P:(t + 1) * P]
                        for half in range(2):
                            n = slice(half * 512, (half + 1) * 512)
                            last = hi_lo(pe, out[:, t % 2, n], *lhs, w_hi[:, k0 + k, n], w_lo[:, k0 + k, n],
                                         k == 0, k == n_k - 1)
                last.then_inc(mm, 1)


def best_keys(nc, A, R):
    with ExitStack() as c:
        sb = lambda n, s, d: c.enter_context(nc.sbuf_tensor(n, s, d))
        sem = lambda n: R.stack.enter_context(nc.semaphore(n))
        KW = KO + 1
        w_st = sb("k_w_st", [P, 2, KW * P], f32)
        w_hi, w_lo = sb("k_w_hi", [P, 2, KO * P], f16), sb("k_w_lo", [P, 2, KO * P], f16)
        k_hi, k_lo = sb("k_k_hi", [P, 2, P], f16), sb("k_k_lo", [P, 2, P], f16)
        q = sb("k_q", [P, 2, NT], f32)
        q_hi, q_lo = sb("k_q_hi", [P, 2, NT], f16), sb("k_q_lo", [P, 2, NT], f16)
        sc = sb("k_sc", [P, 2, TT, P], f32)
        rest = sb("k_rest", [P, TT, P], f32)
        val, idx = sb("k_val", [P, TT, TOPK], f32), sb("k_idx", [P, TT, TOPK], u32)
        ps = c.enter_context(nc.psum_tensor("k_ps", [P, 3, 512], f32))
        ps_s = c.enter_context(nc.psum_tensor("k_ps_s", [P, 3, 512], f32))
        flat_s = ps_s[:].rearrange("p a b -> p (a b)")
        w_in = [sem("k_w_in0"), sem("k_w_in1")]
        k_hi_ok, k_lo_ok = sem("k_k_hi_ok"), sem("k_k_lo_ok")
        w_hi_ok, w_lo_ok, q_mm, q_ev, q_hi_ok, q_lo_ok, s_mm, s_ev, v_ok, i_ok, kept = [sem("k_" + n) for n in
            "w_hi_ok w_lo_ok q_mm q_ev q_hi_ok q_lo_ok s_mm s_ev v_ok i_ok kept".split()]
        block = c.enter_context(nc.Block())

        @block.sync
        def _(sp):
            for m in range(2):
                sp.dma_start(w_st[:, m], A["w_route"][m]).then_inc(w_in[m], 16)
            with sp.Fori(1, HP // 2) as i:
                for s in range(2):
                    sp.wait_ge(w_lo_ok, 2 * i + s - 1)
                    sp.wait_ge(k_lo_ok, 2 * i + s - 1)
                    sp.dma_start(w_st[:, s], A["w_route"][2 * i + s]).then_inc(w_in[s], 16)

        @block.scalar
        def _(act):
            def split_w(m, s, nth, first=False):
                act.wait_ge(w_in[s], nth)
                if not first:
                    act.wait_ge(q_mm, NB * (m - 1))
                act.activation(w_hi[:, s], w_st[:, s, 0:KO * P], ACT.Copy, scale=WSCALE).then_inc(w_hi_ok, 1)

            def split_k(m, s, nth, first=False):
                act.wait_ge(w_in[s], nth)
                if not first:
                    act.wait_ge(s_mm, m - 1)
                act.activation(k_hi[:, s], w_st[:, s, KO * P:], ACT.Copy, scale=WSCALE).then_inc(k_hi_ok, 1)

            def queries(m, s, first=False):
                for b, (t0, n_t) in enumerate(BLOCKS):
                    act.wait_ge(q_mm, NB * m + b + 1)
                    if not first:
                        act.wait_ge(s_mm, m - 1)
                        act.wait_ge(q_lo_ok, m - 1)
                    last = act.activation(q[:, s, t0:t0 + n_t], ps[:, b, 0:n_t], ACT.Copy, scale=1 / WSCALE)
                    last.then_inc(q_ev, 1)
                act.wait_ge(q_ev, NB * m + NB)
                act.activation(q_hi[:, s], q[:, s], ACT.Copy).then_inc(q_hi_ok, 1)

            def scores(m, s, first=False):
                act.wait_ge(s_mm, m + 1)
                if not first:
                    act.wait_ge(kept, m)
                act.activation(sc[:, s].rearrange("p a b -> p (a b)"), flat_s[:, 0:NT], ACT.Copy,
                               scale=1 / WSCALE).then_inc(s_ev, 1)
            split_w(0, 0, 16, True)
            split_w(1, 1, 16, True)
            split_k(0, 0, 16, True)
            queries(0, 0, True)
            split_w(2, 0, 32)
            split_k(1, 1, 16, True)
            queries(1, 1, True)
            split_w(3, 1, 32)
            split_k(2, 0, 32)
            scores(0, 0, True)
            with act.Fori(1, HP // 2 - 1) as i:
                queries(2 * i, 0)
                split_w(2 * i + 2, 0, 16 * i + 32)
                split_k(2 * i + 1, 1, 16 * i + 16)
                scores(2 * i - 1, 1)
                queries(2 * i + 1, 1)
                split_w(2 * i + 3, 1, 16 * i + 32)
                split_k(2 * i + 2, 0, 16 * i + 32)
                scores(2 * i, 0)
            queries(HP - 2, 0)
            split_k(HP - 1, 1, 16 * (HP // 2))
            scores(HP - 3, 1)
            queries(HP - 1, 1)
            scores(HP - 2, 0)
            scores(HP - 1, 1)

        @block.vector
        def _(dve):
            def split_w(m, s):
                dve.wait_ge(w_hi_ok, m + 1)
                dve.scalar_tensor_tensor(w_lo[:, s], w_st[:, s, 0:KO * P], WSCALE, w_hi[:, s], ALU.mult,
                                         ALU.subtract).then_inc(w_lo_ok, 1)

            def split_k(m, s):
                dve.wait_ge(k_hi_ok, m + 1)
                dve.scalar_tensor_tensor(k_lo[:, s], w_st[:, s, KO * P:], WSCALE, k_hi[:, s], ALU.mult,
                                         ALU.subtract).then_inc(k_lo_ok, 1)

            def queries(m, s):
                dve.wait_ge(q_hi_ok, m + 1)
                dve.tensor_tensor(q_lo[:, s], q[:, s], q_hi[:, s], ALU.subtract).then_inc(q_lo_ok, 1)

            def top(m, s):
                wait_apart(dve, s_ev, m + 1)
                wait_apart(dve, kept, m + 1)
                for t in range(TT):
                    last = dve.max(val[:, t, 0:8], sc[:, s, t])
                last.then_inc(v_ok, 1)
                wait_apart(dve, v_ok, 3 * m + 1)
                for t in range(TT):
                    dve.max_index(idx[:, t, 0:8], val[:, t, 0:8], sc[:, s, t])
                    last = dve.match_replace(rest[:, t], val[:, t, 0:8], sc[:, s, t], LOWEST)
                last.then_inc(v_ok, 1)
                wait_apart(dve, v_ok, 3 * m + 2)
                for t in range(TT):
                    last = dve.max(val[:, t, 8:16], rest[:, t])
                last.then_inc(v_ok, 1)
                wait_apart(dve, v_ok, 3 * m + 3)
                for t in range(TT):
                    last = dve.max_index(idx[:, t, 8:16], val[:, t, 8:16], rest[:, t])
                last.then_inc(i_ok, 1)
                dve.wait_ge(i_ok, m + 1)
                dve.tensor_copy(R.top_v[:, m], val[:])
                dve.tensor_copy(R.top_i[:, m], idx[:]).then_inc(kept, 1)
            dve.sem_inc(kept, 1)
            split_w(0, 0)
            split_w(1, 1)
            split_k(0, 0)
            queries(0, 0)
            split_w(2, 0)
            split_k(1, 1)
            queries(1, 1)
            split_w(3, 1)
            split_k(2, 0)
            top(0, 0)
            with dve.Fori(1, HP // 2 - 1) as i:
                queries(2 * i, 0)
                split_w(2 * i + 2, 0)
                split_k(2 * i + 1, 1)
                top(2 * i - 1, 1)
                queries(2 * i + 1, 1)
                split_w(2 * i + 3, 1)
                split_k(2 * i + 2, 0)
                top(2 * i, 0)
            queries(HP - 2, 0)
            split_k(HP - 1, 1)
            top(HP - 3, 1)
            queries(HP - 1, 1)
            top(HP - 2, 0)
            top(HP - 1, 1)

        @block.tensor
        def _(pe):
            def project_half(m, s, first=False):
                pe.wait_ge(w_lo_ok, m + 1)
                for b, (t0, n_t) in enumerate(BLOCKS):
                    if not first:
                        pe.wait_ge(q_ev, NB * m + b - 2)
                    t = slice(t0, t0 + n_t)
                    for k in range(KO):
                        w = slice(k * P, (k + 1) * P)
                        last = hi_lo(pe, ps[:, b, 0:n_t], w_hi[:, s, w], w_lo[:, s, w], R.h_hi[:, k, t],
                                     R.h_lo[:, k, t], k == 0, k == KO - 1)
                    last.then_inc(q_mm, 1)

            def score(m, s, first=False):
                pe.wait_ge(q_lo_ok, m + 1)
                if not first:
                    pe.wait_ge(s_ev, m)
                pe.wait_ge(k_lo_ok, m + 1)
                for t in range(TT):
                    cols = slice(t * P, (t + 1) * P)
                    last = hi_lo(pe, flat_s[:, cols], q_hi[:, s, cols], q_lo[:, s, cols], k_hi[:, s],
                                 k_lo[:, s], True, True)
                last.then_inc(s_mm, 1)
            project_half(0, 0, True)
            project_half(1, 1)
            score(0, 0, True)
            with pe.Fori(1, HP // 2) as i:
                project_half(2 * i, 0)
                score(2 * i - 1, 1)
                project_half(2 * i + 1, 1)
                score(2 * i, 0)
            score(HP - 1, 1)


def best_pairs(nc, A, R):
    with ExitStack() as c:
        sb = lambda n, s, d: c.enter_context(nc.sbuf_tensor(n, s, d))
        sem = lambda n: R.stack.enter_context(nc.semaphore(n))
        NC = TOPK * TOPK
        ident = sb("b_ident", [P, P], f32)
        iota = sb("b_iota", [P, TOPK], f32)
        cand, rest = sb("b_cand", [P, PH, TOPK, TOPK], f32), sb("b_rest", [P, PH, NC], f32)
        best = sb("b_best", [P, PH, TOPK], f32)
        pos = sb("b_pos", [P, PH, TOPK], u32)
        part = sb("b_part", [P, 2, P], u32)
        hit, hit2 = sb("b_hit", [P, P, TOPK], f32), sb("b_hit2", [P, P, TOPK], f32)
        gij = sb("b_gij", [P, 2, 3, P], f32)
        g_tr = sb("b_g_tr", [P, 2, P], f32)
        ex = sb("b_ex", [P, PH, TOPK], f32)
        den = sb("b_den", [P, PH, 2], f32)
        ps = c.enter_context(nc.psum_tensor("b_ps", [P, 2, 512], f32))
        consts, dve_in, dif_ok, exp_ok, gij_ok, t_mm, t_ev, g_hi_ok, g_lo_ok = [sem("b_" + n) for n in
            "consts dve_in dif_ok exp_ok gij_ok t_mm t_ev g_hi_ok g_lo_ok".split()]
        LINKS = 15
        block = c.enter_context(nc.Block())

        @block.sync
        def _(sp):
            sp.dma_start(ident[:], A["ident"]).then_inc(consts, 16)
            sp.dma_start(iota[:], A["iota"][0:TOPK].rearrange("(a n) -> a n", a=1).to_broadcast([P, TOPK])
                         ).then_inc(consts, 16)

        @block.scalar
        def _(act):
            def tile(t, s):
                act.wait_ge(dif_ok, t + 1)
                act.activation(ex[:], ex[:], ACT.Exp).then_inc(exp_ok, 1)
                wait_apart(act, t_mm, t + 1)
                act.activation(g_tr[:, s], ps[:, s, 0:P], ACT.Copy, scale=GSCALE)
                act.activation(R.ij[:, :, bass.ds(t * P, P)], ps[:, s, P:3 * P].rearrange("p (a b) -> p a b", a=2),
                               ACT.Copy).then_inc(t_ev, 1)
                wait_apart(act, t_ev, t + 1)
                act.activation(R.g_hi[:, bass.ds(t * P, P)], g_tr[:, s], ACT.Copy).then_inc(g_hi_ok, 1)
            tile(0, 0)
            tile(1, 1)
            with act.Fori(1, TT // 2) as i:
                act.wait_ge(g_lo_ok, 2 * i - 1)
                tile(2 * i, 0)
                act.wait_ge(g_lo_ok, 2 * i)
                tile(2 * i + 1, 1)

        @block.vector
        def _(dve):
            dve.wait_ge(consts, 32)

            def tile(t, s, peeled):
                count = [0]

                def link(ins):
                    count[0] += 1
                    ins.then_inc(dve_in, 1)
                    wait_apart(dve, dve_in, LINKS * t + count[0])

                first = R.top_v[:, 0::2, t].rearrange("p h (a b) -> p h a b", b=1).to_broadcast([P, PH, TOPK, TOPK])
                second = R.top_v[:, 1::2, t].rearrange("p h (a b) -> p h a b", a=1).to_broadcast([P, PH, TOPK, TOPK])
                link(dve.tensor_tensor(cand[:], first, second, ALU.add))
                rows = [cand[:, h].rearrange("p a b -> p (a b)") for h in range(PH)]
                for h in range(PH):
                    last = dve.max(best[:, h, 0:8], rows[h])
                link(last)
                for h in range(PH):
                    dve.max_index(pos[:, h, 0:8], best[:, h, 0:8], rows[h])
                    last = dve.match_replace(rest[:, h], best[:, h, 0:8], rows[h], LOWEST)
                link(last)
                for h in range(PH):
                    last = dve.max(best[:, h, 8:16], rest[:, h])
                link(last)
                for h in range(PH):
                    last = dve.max_index(pos[:, h, 8:16], best[:, h, 8:16], rest[:, h])
                link(last)
                dve.tensor_tensor(ex[:], best[:], best[:, :, 0:1].to_broadcast([P, PH, TOPK]),
                                  ALU.subtract).then_inc(dif_ok, 1)
                flat = pos[:].rearrange("p h k -> p (h k)")
                dve.tensor_scalar(part[:, 0], flat, 4, None, ALU.logical_shift_right)
                link(dve.tensor_scalar(part[:, 1], flat, TOPK - 1, None, ALU.bitwise_and))
                if not peeled:
                    dve.wait_ge(t_mm, t - 1)
                for half, pick in ((0, hit), (1, hit2)):
                    steps = iota[:].rearrange("p (a n) -> p a n", a=1).to_broadcast([P, P, TOPK])
                    chosen = part[:, half].rearrange("p (n a) -> p n a", a=1).to_broadcast([P, P, TOPK])
                    link(dve.tensor_tensor(pick[:], chosen, steps, ALU.is_equal))
                    names = R.top_i[:, half::2, t].rearrange("p h (b a) -> p h b a", b=1).to_broadcast([P, PH, TOPK, TOPK])
                    picked = pick[:].rearrange("p (h k) a -> p h k a", h=PH)
                    link(dve.tensor_tensor(picked, picked, names, ALU.mult))
                    link(dve.tensor_reduce(gij[:, s, 1 + half], pick[:], AX.X, ALU.add))
                dve.wait_ge(exp_ok, t + 1)
                link(dve.tensor_reduce(den[:, :, 0:1], ex[:], AX.X, ALU.add))
                link(dve.reciprocal(den[:, :, 1:2], den[:, :, 0:1]))
                link(dve.tensor_tensor(gij[:, s, 0].rearrange("p (h k) -> p h k", h=PH), ex[:],
                                       den[:, :, 1:2].to_broadcast([P, PH, TOPK]), ALU.mult))
                dve.tensor_copy(R.soft[:, t], gij[:, s, 0])
                dve.scalar_tensor_tensor(R.expert[:, t], gij[:, s, 1], float(NKEYS), gij[:, s, 2], ALU.mult,
                                         ALU.add).then_inc(gij_ok, 1)
                assert count[0] == LINKS, count

            def g_low(t, s):
                dve.wait_ge(g_hi_ok, t + 1)
                cols = bass.ds(t * P, P)
                dve.tensor_tensor(R.g_lo[:, cols], g_tr[:, s], R.g_hi[:, cols], ALU.subtract).then_inc(g_lo_ok, 1)
            tile(0, 0, True)
            tile(1, 1, True)
            with dve.Fori(1, TT // 2) as i:
                g_low(2 * i - 2, 0)
                tile(2 * i, 0, False)
                g_low(2 * i - 1, 1)
                tile(2 * i + 1, 1, False)
            g_low(TT - 2, 0)
            g_low(TT - 1, 1)

        @block.tensor
        def _(pe):
            pe.wait_ge(consts, 32)

            def tile(t, s, peeled):
                pe.wait_ge(gij_ok, t + 1)
                if not peeled:
                    pe.wait_ge(t_ev, t - 1)
                for a in range(3):
                    last = pe.transpose(ps[:, s, a * P:(a + 1) * P], gij[:, s, a], ident[:])
                last.then_inc(t_mm, 1)
            tile(0, 0, True)
            tile(1, 1, True)
            with pe.Fori(1, TT // 2) as i:
                tile(2 * i, 0, False)
                tile(2 * i + 1, 1, False)


I_GROUP = 4
N_GROUPS = NKEYS // I_GROUP


def dense_gates(nc, A, R):
    with ExitStack() as c:
        sb = lambda n, s, d: c.enter_context(nc.sbuf_tensor(n, s, d))
        sem = lambda n: R.stack.enter_context(nc.semaphore(n))
        OCT, RING, HALF_T, QUAD = 8, 3, 32, 4
        BODY = 2 * HALF_T
        row = sb("g_row", [P, NKEYS], f32)
        iota = sb("g_iota", [P, NKEYS, OCT], f16)
        hot_i, hot_j = sb("g_hot_i", [P, NKEYS, OCT], f16), sb("g_hot_j", [P, RING, NKEYS, OCT], f16)
        hot_g = sb("g_hot_g", [P, RING, 2, NKEYS, OCT], f16)
        out = sb("g_out", [P, 2, N_GROUPS, HALF_T, I_GROUP], f32)
        ps = c.enter_context(nc.psum_tensor("g_ps", [P, 4, QUAD, NKEYS], f32))
        consts, hot_ok, i_ok, mm, ev = [sem("g_" + n) for n in "consts hot_ok i_ok mm ev".split()]
        stored = [sem("g_stored0"), sem("g_stored1")]
        block = c.enter_context(nc.Block())
        NQ, NO = BODY // QUAD, BODY // OCT
        TURNS = 3
        LOOP = (ND // BODY - 1) // TURNS
        REST = [n for n in range(1 + LOOP * TURNS, ND // BODY)]

        def bodies(eng, body):
            body(0, 0, True)
            with eng.Fori(0, LOOP) as i:
                for r in range(TURNS):
                    body(1 + TURNS * i + r, 1 + r, False)
            for n in REST:
                body(n, n, False)

        @block.sync
        def _(sp):
            sp.dma_start(row[:], A["iota"].rearrange("(a n) -> a n", a=1).to_broadcast([P, NKEYS])).then_inc(consts, 16)

            with sp.Fori(0, ND // BODY) as i:
                for h in range(2):
                    sp.wait_ge(ev, NQ * i + NQ // 2 * (h + 1))
                    dst = R.g_dram[:, :, bass.ds(BODY * i + HALF_T * h, HALF_T)].rearrange("g j t f -> j g (t f)")
                    sp.dma_start(dst, out[:, h].rearrange("p g t f -> p g (t f)")).then_inc(stored[h], 16)
            for h in range(2):
                sp.wait_ge(stored[h], 16 * (ND // BODY))

        @block.vector
        def _(dve):
            dve.wait_ge(consts, 16)
            dve.tensor_copy(iota[:], row[:].rearrange("p (n a) -> p n a", a=1).to_broadcast([P, NKEYS, OCT])
                            ).then_inc(i_ok, 1)
            dve.wait_ge(i_ok, 1)

            def body(n, turn, first):
                for o in range(NO):
                    s = (NO * turn + o) % RING
                    toks = bass.ds(BODY * n + OCT * o, OCT)
                    each = lambda ap: ap.rearrange("p (a t) -> p a t", a=1).to_broadcast([P, NKEYS, OCT])
                    dve.tensor_tensor(hot_i[:], iota[:], each(R.ij[:, 0, toks]), ALU.is_equal).then_inc(i_ok, 1)
                    if not first or o >= RING:
                        dve.wait_ge(mm, 2 * (NO * n + o - RING + 1))
                    dve.tensor_tensor(hot_j[:, s], iota[:], each(R.ij[:, 1, toks]), ALU.is_equal)
                    dve.wait_ge(i_ok, NO * n + o + 2)
                    dve.tensor_tensor(hot_g[:, s, 0], hot_i[:], each(R.g_hi[:, toks]), ALU.mult)
                    dve.tensor_tensor(hot_g[:, s, 1], hot_i[:], each(R.g_lo[:, toks]), ALU.mult).then_inc(hot_ok, 1)
                    dve.wait_ge(hot_ok, NO * n + o + 1)
            bodies(dve, body)

        @block.tensor
        def _(pe):
            def body(n, turn, first):
                for q in range(NQ):
                    o, s = q // 2, (NO * turn + q // 2) % RING
                    if not first or q >= 4:
                        pe.wait_ge(ev, NQ * n + q - 3)
                    if q % 2 == 0:
                        pe.wait_ge(hot_ok, NO * n + o + 1)
                    for u in range(QUAD):
                        t = QUAD * (q % 2) + u
                        pe.matmul(ps[:, q % 4, u], hot_j[:, s, :, t], hot_g[:, s, 0, :, t], start=True, stop=False)
                        last = pe.matmul(ps[:, q % 4, u], hot_j[:, s, :, t], hot_g[:, s, 1, :, t], start=False, stop=True)
                    last.then_inc(mm, 1)
            bodies(pe, body)

        @block.scalar
        def _(act):
            def body(n, turn, first):
                for q in range(NQ):
                    h = q // (NQ // 2)
                    t0 = QUAD * (q % (NQ // 2))
                    if q % (NQ // 2) == 0 and not first:
                        act.wait_ge(stored[h], 16 * n)
                    act.wait_ge(mm, NQ * n + q + 1)
                    act.activation(out[:, h, :, t0:t0 + QUAD].rearrange("p g t f -> p t g f"),
                                   ps[:, q % 4].rearrange("p t (g f) -> p t g f", f=I_GROUP), ACT.Copy).then_inc(ev, 1)
            bodies(act, body)


def experts(nc, A, R):
    with ExitStack() as c:
        sb = lambda n, s, d: c.enter_context(nc.sbuf_tensor(n, s, d))
        sem = lambda n: R.stack.enter_context(nc.semaphore(n))
        E = I_GROUP
        VISITS = GT * P // N_GROUPS
        PER_TILE = P // N_GROUPS
        RING = 2
        NBD = len(DENSE)
        u_st, v_st = sb("x_u_st", [P, 2, D], f32), sb("x_v_st", [P, 2, D], f32)
        u_hi, u_lo = sb("x_u_hi", [P, E, KO, P], f16), sb("x_u_lo", [P, E, KO, P], f16)
        v_hi, v_lo = sb("x_v_hi", [P, E, D], f16), sb("x_v_lo", [P, E, D], f16)
        gate = sb("x_gate", [P, ND, E], f32)
        g_act, w = sb("x_g_act", [P, 2, 512], f32), sb("x_w", [P, 2, 512], f32)
        w_hi, w_lo = sb("x_w_hi", [P, E, ND], f16), sb("x_w_lo", [P, E, ND], f16)
        rows = sb("x_rows", [P, RING, 2 * D], f32)
        index = sb("x_index", [P, RING], u32)
        dots, share = sb("x_dots", [P, 2, 2], f32), sb("x_share", [P, 2], f32)
        ps_a = c.enter_context(nc.psum_tensor("x_ps_a", [P, 4, 512], f32))
        ps_v = c.enter_context(nc.psum_tensor("x_ps_v", [P, 2, D], f32))
        u_in = [sem("x_u_in0"), sem("x_u_in1")]
        v_in = [sem("x_v_in0"), sem("x_v_in1")]
        gate_in = [sem(f"x_gate_in{b}") for b in range(NBD)]
        rows_in = [sem(f"x_rows_in{r}") for r in range(RING)]
        u_hi_ok, u_lo_ok, v_hi_ok, v_lo_ok, a_mm, gelu_ok, w_ok, w_hi_ok, w_lo_ok, v_mm, added = [
            sem("x_" + n) for n in "u_hi_ok u_lo_ok v_hi_ok v_lo_ok a_mm gelu_ok w_ok w_hi_ok w_lo_ok v_mm added".split()]
        dot_ok, alive, share_ok, visited, index_ok = [sem("x_" + n) for n in
            "dot_ok alive share_ok visited index_ok".split()]
        A_STEPS = NBD * E
        V_STEPS = DT
        places = [("a", k) for k in range(A_STEPS)] + [("v", t) for t in range(DT)]
        STEPS = len(places)
        AT = {p: (n + 1) * VISITS // STEPS - n * VISITS // STEPS for n, p in enumerate(places)}
        block = c.enter_context(nc.Block())
        u_all, v_all, uv_all = A["peer_u_t"], A["peer_v"], A["peer_uv"]

        @block.sync
        def _(sp):
            def group(i, first):
                for b, (t0, n_t) in enumerate(DENSE):
                    if not first:
                        sp.wait_ge(w_ok, A_STEPS * (i - 1) + E * (b + 1))
                    sp.dma_start(gate[:, t0:t0 + n_t], R.g_dram[i, :, t0:t0 + n_t]).then_inc(gate_in[b], 16)
                for e in range(E):
                    n = E * i + e
                    if not first or e >= 2:
                        sp.wait_ge(u_lo_ok, n - 1)
                    sp.dma_start(u_st[:, e % 2], u_all[n]).then_inc(u_in[e % 2], 16)
                for e in range(E):
                    n = E * i + e
                    if not first or e >= 2:
                        sp.wait_ge(v_lo_ok, n - 1)
                    sp.dma_start(v_st[:, e % 2], v_all[n]).then_inc(v_in[e % 2], 16)
            group(0, True)
            with sp.Fori(1, N_GROUPS) as i:
                group(i, False)

        def visit(i, m):
            return m // PER_TILE, PER_TILE * i + m % PER_TILE

        @block.gpsimd
        def _(pool):
            def group(i, first):
                for m in range(VISITS):
                    tile, hk = visit(i, m)
                    if not first or m >= RING:
                        wait_apart(pool, visited, VISITS * i + m - RING + 1)
                    pool.tensor_copy(index[:, m % RING:m % RING + 1],
                                     R.expert[:, DT + tile, bass.ds(hk, 1)]).then_inc(index_ok, 1)
                    wait_apart(pool, index_ok, VISITS * i + m + 1)
                    pool.indirect_dma_start(rows[:, m % RING], None, uv_all,
                                            bass.IndirectOffsetOnAxis(ap=index[:, m % RING:m % RING + 1], axis=0)
                                            ).then_inc(rows_in[m % RING], 16)
            group(0, True)
            with pool.Fori(1, N_GROUPS) as i:
                group(i, False)

        @block.scalar
        def _(act):
            def group(i, first):
                m = [0]

                def visits(place):
                    for _ in range(AT[place]):
                        tile, hk = visit(i, m[0])
                        n, s = VISITS * i + m[0], m[0] % 2
                        act.wait_ge(dot_ok, n + 1)
                        act.activation(dots[:, s, 1:2], dots[:, s, 0:1], ACT.Gelu).then_inc(alive, 1)
                        if not first or m[0] >= 2:
                            act.wait_ge(visited, n - 1)
                        wait_apart(act, alive, n + 1)
                        act.activation(share[:, s:s + 1], dots[:, s, 1:2], ACT.Copy,
                                       scale=R.soft[:, DT + tile, bass.ds(hk, 1)]).then_inc(share_ok, 1)
                        m[0] += 1

                for e in range(E):
                    act.wait_ge(u_in[e % 2], 32 * i + 16 * (e // 2 + 1))
                    if not first:
                        act.wait_ge(a_mm, A_STEPS * i - E + e + 1)
                    act.activation(u_hi[:, e].rearrange("p a b -> p (a b)"), u_st[:, e % 2], ACT.Copy,
                                   scale=WSCALE).then_inc(u_hi_ok, 1)

                def high(n, slot, e, t0, n_t):
                    act.wait_ge(w_ok, n + 1)
                    act.activation(w_hi[:, e, t0:t0 + n_t], w[:, slot, 0:n_t], ACT.Copy).then_inc(w_hi_ok, 1)
                before = None
                for b, (t0, n_t) in enumerate(DENSE):
                    for e in range(E):
                        k = E * b + e
                        n = A_STEPS * i + k
                        act.wait_ge(a_mm, n + 1)
                        if not first or k >= 2:
                            act.wait_ge(w_ok, n - 1)
                        act.activation(g_act[:, k % 2, 0:n_t], ps_a[:, k % 4, 0:n_t], ACT.Gelu,
                                       scale=1 / WSCALE).then_inc(gelu_ok, 1)
                        if before:
                            high(n - 1, (k - 1) % 2, *before)
                        before = (e, t0, n_t)
                        if b == 0:
                            act.wait_ge(v_in[e % 2], 32 * i + 16 * (e // 2 + 1))
                            if not first:
                                act.wait_ge(v_mm, V_STEPS * i)
                            act.activation(v_hi[:, e], v_st[:, e % 2], ACT.Copy, scale=VSCALE).then_inc(v_hi_ok, 1)
                        visits(("a", k))
                high(n, k % 2, *before)
                for t in range(DT):
                    visits(("v", t))
            group(0, True)
            with act.Fori(1, N_GROUPS) as i:
                group(i, False)

        @block.vector
        def _(dve):
            def use(n, s, r, tile):
                dve.wait_ge(share_ok, n + 1)
                dve.scalar_tensor_tensor(R.acc[:, DT + tile], rows[:, r, D:2 * D], share[:, s:s + 1],
                                         R.acc[:, DT + tile], ALU.mult, ALU.add).then_inc(visited, 1)

            def group(i, first):
                m = [0]

                def visits(place):
                    for _ in range(AT[place]):
                        k = m[0]
                        tile, _hk = visit(i, k)
                        n = VISITS * i + k
                        dve.wait_ge(rows_in[k % RING], 16 * (VISITS // RING) * i + 16 * (k // RING + 1))
                        dve.tensor_tensor_reduce(out=rows[:, k % RING, 0:D], in0=R.h_nat[:, tile], in1=rows[:, k % RING, 0:D],
                                                 scale=1.0, scalar=0.0, op0=ALU.mult, op1=ALU.add,
                                                 accum_out=dots[:, k % 2, 0:1]).then_inc(dot_ok, 1)
                        if not first or k:
                            if not first or k >= 2:
                                dve.wait_ge(visited, n - 1)
                            use(n - 1, (k - 1) % 2, (k - 1) % RING, visit(i, k - 1)[0] if k else GT - 1)
                        m[0] += 1

                for e in range(E):
                    dve.wait_ge(u_hi_ok, E * i + e + 1)
                    dve.scalar_tensor_tensor(u_lo[:, e].rearrange("p a b -> p (a b)"), u_st[:, e % 2], WSCALE,
                                             u_hi[:, e].rearrange("p a b -> p (a b)"), ALU.mult,
                                             ALU.subtract).then_inc(u_lo_ok, 1)

                def low(n, slot, e, t0, n_t):
                    dve.wait_ge(w_hi_ok, n + 1)
                    dve.tensor_tensor(w_lo[:, e, t0:t0 + n_t], w[:, slot, 0:n_t], w_hi[:, e, t0:t0 + n_t],
                                      ALU.subtract).then_inc(w_lo_ok, 1)
                before = None
                for b, (t0, n_t) in enumerate(DENSE):
                    dve.wait_ge(gate_in[b], 16 * i + 16)
                    for e in range(E):
                        k = E * b + e
                        n = A_STEPS * i + k
                        dve.wait_ge(gelu_ok, n + 1)
                        if not first or k >= 2:
                            dve.wait_ge(w_lo_ok, n - 1)
                        dve.tensor_tensor(w[:, k % 2, 0:n_t], g_act[:, k % 2, 0:n_t], gate[:, t0:t0 + n_t, e],
                                          ALU.mult).then_inc(w_ok, 1)
                        if before:
                            low(n - 1, (k - 1) % 2, *before)
                        before = (e, t0, n_t)
                        if b == 0:
                            dve.wait_ge(v_hi_ok, E * i + e + 1)
                            dve.scalar_tensor_tensor(v_lo[:, e], v_st[:, e % 2], VSCALE, v_hi[:, e], ALU.mult,
                                                     ALU.subtract).then_inc(v_lo_ok, 1)
                        visits(("a", k))
                low(n, k % 2, *before)
                for t in range(DT):
                    visits(("v", t))
                    dve.wait_ge(v_mm, V_STEPS * i + t + 1)
                    dve.scalar_tensor_tensor(R.acc[:, t], ps_v[:, t % 2], 1 / (VSCALE * GSCALE), R.acc[:, t],
                                             ALU.mult, ALU.add).then_inc(added, 1)
            group(0, True)
            with dve.Fori(1, N_GROUPS) as i:
                group(i, False)
            last = N_GROUPS * VISITS - 1
            dve.wait_ge(visited, last)
            use(last, (VISITS - 1) % 2, (VISITS - 1) % RING, GT - 1)

        @block.tensor
        def _(pe):
            def group(i, first):
                def a_block(b):
                    t0, n_t = DENSE[b]
                    t = slice(t0, t0 + n_t)
                    for e in range(E):
                        k = E * b + e
                        n = A_STEPS * i + k
                        out = ps_a[:, k % 4, 0:n_t]
                        if not first or k >= 4:
                            pe.wait_ge(gelu_ok, n - 3)
                        if b == 0:
                            pe.wait_ge(u_hi_ok, E * i + e + 1)
                        for ko in range(KO):
                            pe.matmul(out, u_hi[:, e, ko], R.h_hi[:, ko, t], start=ko == 0, stop=False)
                            pe.matmul(out, u_hi[:, e, ko], R.h_lo[:, ko, t], start=False, stop=False)
                        if b == 0:
                            pe.wait_ge(u_lo_ok, E * i + e + 1)
                        for ko in range(KO):
                            last = pe.matmul(out, u_lo[:, e, ko], R.h_hi[:, ko, t], start=False, stop=ko == KO - 1)
                        last.then_inc(a_mm, 1)

                def v_block(b):
                    t0, n_t = DENSE[b]
                    pe.wait_ge(w_lo_ok, A_STEPS * i + E * (b + 1))
                    if b == 0:
                        pe.wait_ge(v_lo_ok, E * (i + 1))
                    for t in range(t0 // P, (t0 + n_t) // P):
                        if not first or t >= 2:
                            pe.wait_ge(added, V_STEPS * i + (t - 1 if DT % 2 == 0 or t else 0))
                        cols = slice(t * P, (t + 1) * P)
                        for e in range(E):
                            for half in range(2):
                                d = slice(half * 512, (half + 1) * 512)
                                last = hi_lo(pe, ps_v[:, t % 2, d], w_hi[:, e, cols], w_lo[:, e, cols],
                                             v_hi[:, e, d], v_lo[:, e, d], e == 0, e == E - 1)
                        last.then_inc(v_mm, 1)
                for b in range(NBD):
                    a_block(b)
                for b in range(NBD):
                    v_block(b)
            group(0, True)
            with pe.Fori(1, N_GROUPS) as i:
                group(i, False)


def final_norm(nc, A, R, outs):
    with ExitStack() as c:
        sb = lambda n, s, d: c.enter_context(nc.sbuf_tensor(n, s, d))
        sem = lambda n: R.stack.enter_context(nc.semaphore(n))
        gain, shift = sb("n_gain", [P, D], f32), sb("n_shift", [P, D], f32)
        stats, mv = sb("n_stats", [P, 2, 6], f32), sb("n_mv", [P, 4], f32)
        consts, v_ok, sq_ok, y_ok, dve_in, stored = [sem("n_" + n) for n in "consts v_ok sq_ok y_ok dve_in stored".split()]
        block = c.enter_context(nc.Block())

        @block.sync
        def _(sp):
            sp.dma_start(gain[:], A["ln2_g"].to_broadcast([P, D])).then_inc(consts, 16)
            sp.dma_start(shift[:], A["ln2_b"].to_broadcast([P, D])).then_inc(consts, 16)
            for t in range(TT):
                sp.wait_ge(y_ok, t + 1)
                k = t * P
                dst = outs[0][0, k:k + P] if k < SEQS[0] else outs[1][0, k - SEQS[0]:k - SEQS[0] + P]
                sp.dma_start(dst, R.acc[:, t]).then_inc(stored, 16)
            sp.wait_ge(stored, 16 * TT)

        @block.scalar
        def _(act):
            for t in range(TT):
                act.wait_ge(v_ok, t + 1)
                act.activation(mv[:, 2:3], mv[:, 2:3], ACT.Sqrt).then_inc(sq_ok, 1)

        @block.vector
        def _(dve):
            link = linker(dve, dve_in)
            dve.wait_ge(consts, 32)
            for t in range(TT):
                layer_norm_steps(dve, R.acc[:, t], stats, mv, gain[:], shift[:], link, v_ok, sq_ok, t).then_inc(y_ok, 1)


def build(nc, A, outs):
    R = Buffers()
    R.stack = ExitStack()
    with R.stack:
        R.x_hi_dram = nc.dram_tensor("x_hi_scratch", [P, KO, NT], f16).ap()
        R.x_lo_dram = nc.dram_tensor("x_lo_scratch", [P, KO, NT], f16).ap()
        R.g_dram = nc.dram_tensor("gate_scratch", [N_GROUPS, P, ND, I_GROUP], f32).ap()
        with ExitStack() as branches:
            right = lambda n, s, d: branches.enter_context(nc.sbuf_tensor(n, s, d, side="right"))
            with ExitStack() as inputs:
                left = lambda n, s, d: inputs.enter_context(nc.sbuf_tensor(n, s, d))
                R.proj = left("proj", [P, NM, NT], f32)
                values = ExitStack()
                R.v = values.enter_context(nc.sbuf_tensor("v", [P, TT, HEADS * DV], f32))
                project(nc, A, R)
                R.o_hi, R.o_lo = right("o_hi", [P, HEADS, NT], f16), right("o_lo", [P, HEADS, NT], f16)
                gated_attention(nc, A, R)
                values.close()
                R.f_hi, R.f_lo = right("f_hi", [P, GROUPS, NT], f16), right("f_lo", [P, GROUPS, NT], f16)
                fourier(nc, A, R)
            merged = ExitStack()
            R.m_hi = merged.enter_context(nc.sbuf_tensor("m_hi", [P, KO, NT], f16))
            R.m_lo = merged.enter_context(nc.sbuf_tensor("m_lo", [P, KO, NT], f16))
            merge(nc, A, R)
        with ExitStack() as tail:
            right = lambda n, s, d: tail.enter_context(nc.sbuf_tensor(n, s, d, side="right"))
            R.h_hi, R.h_lo = right("h_hi", [P, KO, NT], f16), right("h_lo", [P, KO, NT], f16)
            R.acc = right("acc", [P, TT, D], f32)
            R.h_nat = right("h_nat", [P, GT, D], f32)
            R.expert, R.soft = right("expert", [P, TT, P], u32), right("soft", [P, TT, P], f32)
            mix_norm(nc, A, R)
            merged.close()
            embed(nc, A, R)
            with ExitStack() as routing:
                routed = lambda n, s: routing.enter_context(nc.sbuf_tensor(n, s, f16, side="right"))
                R.ij, R.g_hi, R.g_lo = routed("ij", [P, 2, NT]), routed("g_hi", [P, NT]), routed("g_lo", [P, NT])
                with ExitStack() as tops:
                    R.top_v = tops.enter_context(nc.sbuf_tensor("top_v", [P, HP, TT, TOPK], f32))
                    R.top_i = tops.enter_context(nc.sbuf_tensor("top_i", [P, HP, TT, TOPK], f32))
                    best_keys(nc, A, R)
                    best_pairs(nc, A, R)
                dense_gates(nc, A, R)
            experts(nc, A, R)
            final_norm(nc, A, R, outs)


def _halves(table):
    hi = (table * WSCALE).astype(np.float16)
    return hi, (table * WSCALE - hi.astype(np.float64)).astype(np.float16)


def _dft(n):
    k = np.arange(n)
    angle = 2 * np.pi * (np.outer(k, k) % n) / n
    return np.cos(angle), np.sin(angle)


def _tables():
    cos_c, sin_c = _dft(GDIM)
    t = {"dft_c": np.stack(_halves(np.concatenate([cos_c, sin_c], 1)), 1)}
    for name, n in (("dft_t", SEQS[0]), ("dft_s", SEQS[1])):
        cos_t, sin_t = _dft(n)
        parts = np.stack([np.stack(_halves(cos_t)), np.stack(_halves(-sin_t))])
        t[name] = np.ascontiguousarray(parts.reshape(2, 2, n // P, P, n).transpose(3, 0, 1, 2, 4))
    s, q = np.arange(P)[:, None], np.arange(P)[None, :]
    same = s // CHUNK == q // CHUNK
    t["causal"] = np.stack([same & (s <= q), same & (s > q)], 1).astype(np.float32)
    t["ident"] = np.eye(P, dtype=np.float32)
    t["iota"] = np.arange(NKEYS, dtype=np.float32)
    return t


def _column_tiles(w):
    k, n = w.shape
    return np.ascontiguousarray(w.reshape(k // P, P, n // P, P).transpose(2, 1, 0, 3).reshape(n // P, P, k))


def _layout(x):
    a = {k: np.asarray(v) for k, v in x.items()}
    L = _tables()
    tokens = np.concatenate([a["x_prompt"][0], a["x_sample"][0]], 0)
    L["x"] = tokens.reshape(TT, P, D)
    L["x_t"] = np.ascontiguousarray(tokens.T).reshape(KO, P, NT)
    p = np.concatenate([a["p_prompt"][0, 0], a["p_sample"][0, 0]], 0)
    L["p_t"] = np.ascontiguousarray(p.T.reshape(PLE // P, P, NT).transpose(1, 0, 2))
    w = a["w_in"][0]
    qk, vw = HEADS * DK, HEADS * DV
    q, k, v, r = w[:, :qk], w[:, qk:2 * qk], w[:, 2 * qk:2 * qk + vw], w[:, 2 * qk + vw:2 * qk + 2 * vw]
    low = w[:, 2 * qk + 2 * vw:2 * qk + 2 * vw + 2 * RANK]
    f = w[:, 2 * qk + 2 * vw + 2 * RANK:]
    rest = np.zeros((D, P), np.float32)
    rest[:, 0:RANK], rest[:, AB_ROW:AB_ROW + RANK] = low[:, :RANK], low[:, RANK:]
    L["w_proj"] = _column_tiles(np.concatenate([rest, q, k, r, f], 1))
    L["w_v"] = np.ascontiguousarray(v.reshape(4, 2, P, vw).transpose(0, 2, 1, 3).reshape(4, P, 2 * vw))
    a2 = np.zeros((2 * AB_ROW, qk), np.float32)
    a2[0:RANK], a2[AB_ROW:AB_ROW + RANK] = a["w_af2"][0], a["w_ab2"][0]
    L["w_a2"] = a2
    L["b_a"] = np.ascontiguousarray(np.stack([a["b_af"][0].reshape(PAIRS, P), a["b_ab"][0].reshape(PAIRS, P)], 1)
                                    .reshape(2 * PAIRS, P).T)
    L["norm_g"] = a["gla_norm_g"][0].reshape(P, 1)
    mg = _column_tiles(a["w_mg"][0])
    L["w_merge"] = np.concatenate([mg[:KO], mg[KO:], _column_tiles(a["w_ao"][0]), _column_tiles(a["w_fo"][0])], 2)
    L["b_mg"] = np.ascontiguousarray(a["b_mg"][0].reshape(2, KO, P).transpose(2, 0, 1))
    L["w_o"] = a["w_o"][0].reshape(KO, P, D)
    L["w_ple"] = np.concatenate([a["w_pg"][0].reshape(KO, P, D), a["w_pe"][0].reshape(PLE // P, P, D)], 0)
    keys = a["peer_keys"][0].reshape(HP, NKEYS, HALF).transpose(0, 2, 1)
    L["w_route"] = np.concatenate([_column_tiles(a["w_pq"][0]), keys], 2)
    L["peer_u_t"] = _column_tiles(np.ascontiguousarray(a["peer_u"][0].T))
    L["peer_v"] = a["peer_v"][0].reshape(EXPERTS // P, P, D)
    L["peer_uv"] = np.concatenate([a["peer_u"][0], a["peer_v"][0]], 1)
    for n in ("ln1_g", "ln1_b", "ln2_g", "ln2_b"):
        L[n] = a[n][0].reshape(1, D)
    return L


def kernel(**inputs):
    import concourse.bacc as bacc
    from concourse.bass_utils import run_bass_kernel_spmd

    nc = bacc.Bacc("TRN2", target_bir_lowering=False, num_devices=1)
    arrays = {n: np.ascontiguousarray(a) for n, a in _layout(inputs).items()}
    A = {n: nc.dram_tensor("in_" + n, a.shape, mybir.dt.from_np(a.dtype), kind="ExternalInput").ap()
         for n, a in arrays.items()}
    outs = [nc.dram_tensor(f"out_{i}", (1, n, D), f32, kind="ExternalOutput").ap() for i, n in enumerate(SEQS)]
    build(nc, A, outs)
    r = run_bass_kernel_spmd(nc, [{"in_" + n: a for n, a in arrays.items()}], core_ids=[0])
    return r.results[0]["out_0"], r.results[0]["out_1"]
```

```python
from contextlib import ExitStack

import concourse.bass as bass
import numpy as np
from concourse import mybir

f32 = mybir.dt.float32
f16 = mybir.dt.float16
u32 = mybir.dt.uint32
ALU = mybir.AluOpType
ACT = mybir.ActivationFunctionType
AX = mybir.AxisListType

P = 128
SEQS = (1024, 256)
NT = sum(SEQS)
TT = NT // P
BLOCKS = ((0, 512), (512, 512), (1024, 256))
NB = len(BLOCKS)
D = 1024
KO = D // P
HEADS, DK, DV, RANK, CHUNK = 4, 64, 128, 16, 64
NCH = NT // CHUNK
PAIRS = HEADS * DK // P
GROUPS, GDIM = 4, 128
PH, NKEYS, TOPK, HALF = 8, 128, 16, 128
HP = PH * 2
EXPERTS = NKEYS * NKEYS
GT = 4
DT = TT - GT
ND = DT * P
DENSE = tuple((t0, min(512, ND - t0)) for t0 in range(0, ND, 512))
PLE = 256
LN_EPS, RMS_EPS = 1e-5, 1e-6
ALPHA = 2.0 ** 0.25
WSCALE = 64.0
VSCALE = 4.0
GSCALE = 256.0
LOWEST = -3.0e38

M_Q, M_K, M_R, M_F, M_LOW, NM = 0, 2, 4, 8, 12, 13
AB_ROW = 32


def hi_lo(pe, out, lhs_hi, lhs_lo, rhs_hi, rhs_lo, first, last):
    pe.matmul(out, lhs_hi, rhs_hi, start=first, stop=False)
    pe.matmul(out, lhs_hi, rhs_lo, start=False, stop=False)
    return pe.matmul(out, lhs_lo, rhs_hi, start=False, stop=last)


def wait_apart(eng, sem, value):
    eng.wait_ge(sem, value)
    eng.nop(nofuse=True)


def project(nc, A, R):
    with ExitStack() as c:
        sb = lambda n, s, d: c.enter_context(nc.sbuf_tensor(n, s, d))
        sem = lambda n: R.stack.enter_context(nc.semaphore(n))
        x_hi, x_lo = sb("p_x_hi", [P, KO, NT], f16), sb("p_x_lo", [P, KO, NT], f16)
        x_st = sb("p_x_st", [P, 2, NT], f32)
        w_st = sb("p_w_st", [P, 2, D], f32)
        w_hi, w_lo = sb("p_w_hi", [P, 2, KO, P], f16), sb("p_w_lo", [P, 2, KO, P], f16)
        v_hi, v_lo = sb("p_v_hi", [P, KO, 512], f16), sb("p_v_lo", [P, KO, 512], f16)
        ps = c.enter_context(nc.psum_tensor("p_ps", [P, 2, 3, 512], f32))
        psv = c.enter_context(nc.psum_tensor("p_psv", [P, 2, 512], f32))
        x_in = [sem("p_x_in0"), sem("p_x_in1")]
        w_in = [sem("p_w_in0"), sem("p_w_in1")]
        x_hi_ok, x_lo_ok, w_hi_ok, w_lo_ok = sem("p_x_hi_ok"), sem("p_x_lo_ok"), sem("p_w_hi_ok"), sem("p_w_lo_ok")
        v_mm, v_ev, m_mm, m_ev, stored = sem("p_v_mm"), sem("p_v_ev"), sem("p_m_mm"), sem("p_m_ev"), sem("p_stored")
        NV = 4

        block = c.enter_context(nc.Block())

        @block.sync
        def _(sp):
            def load(s, slot, src):
                if isinstance(s, int) and s < 2:
                    pass
                else:
                    sp.wait_ge(w_lo_ok, s - 1)
                sp.dma_start(w_st[:, slot], src).then_inc(w_in[slot], 16)

            for k in range(KO):
                if k >= 2:
                    sp.wait_ge(x_lo_ok, k - 1)
                sp.dma_start(x_st[:, k % 2], A["x_t"][k]).then_inc(x_in[k % 2], 16)
                if k < 2:
                    load(k, k, A["w_v"][k])
            load(2, 0, A["w_v"][2])
            load(3, 1, A["w_v"][3])
            load(NV, 0, A["w_proj"][0])
            with sp.Fori(0, 6) as i:
                load(NV + 1 + 2 * i, 1, A["w_proj"][1 + 2 * i])
                load(NV + 2 + 2 * i, 0, A["w_proj"][2 + 2 * i])
            sp.wait_ge(x_hi_ok, KO)
            sp.wait_ge(x_lo_ok, KO)
            sp.dma_start(R.x_hi_dram, x_hi[:]).then_inc(stored, 16)
            sp.dma_start(R.x_lo_dram, x_lo[:]).then_inc(stored, 16)
            sp.wait_ge(stored, 32)

        def m_items(eng, body):
            body(eng, 0, 0, M_LOW, True)
            with eng.Fori(0, 6) as i:
                body(eng, 1 + 2 * i, 1, 2 * i, False)
                body(eng, 2 + 2 * i, 0, 2 * i + 1, False)

        @block.scalar
        def _(act):
            for k in range(KO):
                act.wait_ge(x_in[k % 2], 16 * (k // 2 + 1))
                act.activation(x_hi[:, k], x_st[:, k % 2], ACT.Copy).then_inc(x_hi_ok, 1)
                if k < 2:
                    act.wait_ge(w_in[k], 16)
                    act.activation(v_hi[:, 2 * k:2 * k + 2].rearrange("p a b -> p (a b)"), w_st[:, k],
                                   ACT.Copy, scale=WSCALE).then_inc(w_hi_ok, 1)
            for k in range(2, NV):
                act.wait_ge(w_in[k % 2], 32)
                act.activation(v_hi[:, 2 * k:2 * k + 2].rearrange("p a b -> p (a b)"), w_st[:, k % 2],
                               ACT.Copy, scale=WSCALE).then_inc(w_hi_ok, 1)

            def w_split(n, slot, nth):
                act.wait_ge(w_in[slot], 16 * nth)
                if not isinstance(n, int) or n >= 2:
                    act.wait_ge(m_mm, 3 * n - 3)
                act.activation(w_hi[:, slot].rearrange("p a b -> p (a b)"), w_st[:, slot], ACT.Copy,
                               scale=WSCALE).then_inc(w_hi_ok, 1)

            def evacuate(n, slot, m):
                for b, (t0, n_t) in enumerate(BLOCKS):
                    wait_apart(act, m_mm, 3 * n + b + 1)
                    act.activation(R.proj[:, m, t0:t0 + n_t], ps[:, slot, b, 0:n_t], ACT.Copy,
                                   scale=1 / WSCALE).then_inc(m_ev, 1)

            w_split(0, 0, 3)
            for t in range(TT):
                act.wait_ge(v_mm, t + 1)
                act.activation(R.v[:, t], psv[:, t % 2], ACT.Copy, scale=1 / WSCALE).then_inc(v_ev, 1)
            w_split(1, 1, 3)
            evacuate(0, 0, M_LOW)
            with act.Fori(0, 5) as i:
                w_split(2 + 2 * i, 0, i + 4)
                evacuate(1 + 2 * i, 1, 2 * i)
                w_split(3 + 2 * i, 1, i + 4)
                evacuate(2 + 2 * i, 0, 2 * i + 1)
            w_split(12, 0, 9)
            evacuate(11, 1, 10)
            evacuate(12, 0, 11)

        @block.vector
        def _(dve):
            def v_lo_part(k):
                dve.wait_ge(w_hi_ok, k + 1)
                dve.scalar_tensor_tensor(v_lo[:, 2 * k:2 * k + 2].rearrange("p a b -> p (a b)"), w_st[:, k % 2],
                                         WSCALE, v_hi[:, 2 * k:2 * k + 2].rearrange("p a b -> p (a b)"),
                                         ALU.mult, ALU.subtract).then_inc(w_lo_ok, 1)
            for k in range(KO):
                dve.wait_ge(x_hi_ok, k + 1)
                dve.tensor_tensor(x_lo[:, k], x_st[:, k % 2], x_hi[:, k], ALU.subtract).then_inc(x_lo_ok, 1)
                if k < 2:
                    v_lo_part(k)
            for k in range(2, NV):
                v_lo_part(k)

            def w_split(eng, n, slot, m, first):
                eng.wait_ge(w_hi_ok, n + NV + 1)
                eng.scalar_tensor_tensor(w_lo[:, slot].rearrange("p a b -> p (a b)"), w_st[:, slot], WSCALE,
                                         w_hi[:, slot].rearrange("p a b -> p (a b)"),
                                         ALU.mult, ALU.subtract).then_inc(w_lo_ok, 1)
            m_items(dve, w_split)

        @block.tensor
        def _(pe):
            pe.wait_ge(w_lo_ok, NV)
            for t in range(TT):
                if t >= 2:
                    pe.wait_ge(v_ev, t - 1)
                for k in range(KO):
                    if t == 0:
                        pe.wait_ge(x_lo_ok, k + 1)
                    last = hi_lo(pe, psv[:, t % 2], x_hi[:, k, t * P:(t + 1) * P], x_lo[:, k, t * P:(t + 1) * P],
                                 v_hi[:, k], v_lo[:, k], k == 0, k == KO - 1)
                last.then_inc(v_mm, 1)

            def tile(eng, n, slot, m, first):
                eng.wait_ge(w_lo_ok, n + NV + 1)
                for b, (t0, n_t) in enumerate(BLOCKS):
                    if not first:
                        eng.wait_ge(m_ev, 3 * n + b - 2)
                    for k in range(KO):
                        last = hi_lo(eng, ps[:, slot, b, 0:n_t], w_hi[:, slot, k], w_lo[:, slot, k],
                                     x_hi[:, k, t0:t0 + n_t], x_lo[:, k, t0:t0 + n_t], k == 0, k == KO - 1)
                    last.then_inc(m_mm, 1)
            m_items(pe, tile)


class Buffers:
    pass


def gated_attention(nc, A, R):
    with ExitStack() as c:
        sb = lambda n, s, d: c.enter_context(nc.sbuf_tensor(n, s, d))
        sem = lambda n: R.stack.enter_context(nc.semaphore(n))
        w_a2 = sb("a_w_a2", [2 * AB_ROW, HEADS * DK], f32)
        b_a = sb("a_b_a", [P, 4], f32)
        norm_g = sb("a_norm_g", [P, 1], f32)
        causal = sb("a_causal", [P, 2, P], f32)
        ident = sb("a_ident", [P, P], f32)
        ones = sb("a_ones", [P, P], f32)
        reset = sb("a_reset", [P, NT], f16)
        z = sb("a_z", [P, NT], f32)
        soft = sb("a_soft", [P, NT], f32)
        cums = sb("a_cum", [P, 2, NT], f32)
        kk = sb("a_kk", [P, NT], f32)
        k_st = sb("a_k_st", [P, NT], f32)
        qq = sb("a_qq", [P, NT], f32)
        q_in = sb("a_q_in", [P, 2, NT], f32)
        k_nat = sb("a_k_nat", [P, TT, P], f32)
        probs = sb("a_probs", [P, 2, 2, TT, P], f32)
        state = sb("a_state", [P, 2, NCH, DV], f32)
        o_sb, o_sq, o_g, rms = z, soft, kk, qq
        ps_z = c.enter_context(nc.psum_tensor("a_ps_z", [P, 3, 512], f32))
        ps_x = c.enter_context(nc.psum_tensor("a_ps_x", [P, 3, 512], f32))
        ps_d = c.enter_context(nc.psum_tensor("a_ps_d", [P, 2, 4, DV], f32))
        flat_z = ps_z[:].rearrange("p a b -> p (a b)")
        flat_x = ps_x[:].rearrange("p a b -> p (a b)")

        consts, z_mm, z_ok, soft_ok, cum_ok, e_ok, gated = [sem("a_" + n) for n in
            "consts z_mm z_ok soft_ok cum_ok e_ok gated".split()]
        kt_mm, kt_ev, s_mm, s_ev, d_mm, st_ok, o_mm, o_ev = [sem("a_" + n) for n in
            "kt_mm kt_ev s_mm s_ev d_mm st_ok o_mm o_ev".split()]
        ms_mm, rms_ok, rec_ok, o_res, o_hi_ok, o_lo_ok, silu_ok, made, act_in, dve_in = [sem("a_" + n) for n in
            "ms_mm rms_ok rec_ok o_res o_hi_ok o_lo_ok silu_ok made act_in dve_in".split()]
        UNITS = [(pr, dr) for pr in range(PAIRS) for dr in range(2)]
        n0 = SEQS[0] // CHUNK
        ORDER = [[list(range(n0)), list(range(n0, NCH))], [list(range(n0 - 1, -1, -1)), list(range(NCH - 1, n0 - 1, -1))]]
        STEPS = [[(a, b) for seq in ORDER[dr] for a, b in zip(seq, seq[1:])] for dr in range(2)]
        NS = len(STEPS[0])
        FIRST = [[seq[0] for seq in ORDER[dr]] for dr in range(2)]
        LAST_C, MID_C = (CHUNK - 1, 0), (CHUNK // 2 - 1, CHUNK - CHUNK // 2)
        SLOT, BATCH = [], []
        for dr in range(2):
            SLOT.append([])
            BATCH.append([])
            used = [4, 4]
            for k, (a, _) in enumerate(STEPS[dr]):
                if used[a % 2] == 4:
                    used = [0, 0]
                    BATCH[dr].append(k)
                SLOT[dr].append((len(BATCH[dr]) - 1, a % 2, used[a % 2]))
                used[a % 2] += 1
            BATCH[dr].append(NS)

        def delta(dr, k):
            batch, bank, slot = SLOT[dr][k]
            if batch % 2:
                return ps_z[:, bank, slot * DV:(slot + 1) * DV]
            return ps_d[:, bank, slot]

        def by_chunk(ap, at):
            v = ap.rearrange("p (n c) -> p n c", c=CHUNK)
            return v, v[:, :, at:at + 1].to_broadcast([P, NCH, CHUNK])

        block = c.enter_context(nc.Block())

        @block.sync
        def _(sp):
            for dst, src in ((w_a2, "w_a2"), (b_a, "b_a"), (norm_g, "norm_g"), (causal, "causal"), (ident, "ident")):
                sp.dma_start(dst[:], A[src]).then_inc(consts, 16)

        @block.scalar
        def _(act):
            r_all = R.proj[:, M_R:M_R + 4].rearrange("p a b -> p (a b)")
            act.activation(r_all, r_all, ACT.Silu).then_inc(silu_ok, 1)
            act.wait_ge(consts, 16 * 5)

            def gate(u):
                act.wait_ge(z_mm, u + 1)
                if u:
                    act.wait_ge(cum_ok, u)
                if u == 2:
                    act.wait_ge(o_res, 2)
                z_ps = (flat_z, flat_x)[u % 2]
                act.activation(z[:], z_ps[:, 0:NT], ACT.Identity, bias=b_a[:, u:u + 1]).then_inc(z_ok, 1)
                act.wait_ge(z_ok, u + 1)
                act.activation(soft[:], z[:], ACT.Abs).then_inc(act_in, 1)
                act.wait_ge(act_in, 2 * u + 1)
                act.activation(soft[:], soft[:], ACT.Exp, scale=-1.0).then_inc(act_in, 1)
                act.wait_ge(act_in, 2 * u + 2)
                act.activation(soft[:], soft[:], ACT.Ln, bias=1.0).then_inc(soft_ok, 1)
                act.wait_ge(cum_ok, u + 1)
                act.activation(qq[:], kk[:], ACT.Exp, scale=1 / 16)
                act.activation(kk[:], kk[:], ACT.Exp, scale=-1 / 16)
                act.activation(cums[:, u % 2], cums[:, u % 2], ACT.Exp, scale=1 / 16)
                act.activation(k_st[:], k_st[:], ACT.Exp, scale=1 / 16).then_inc(e_ok, 1)

            def keys(u):
                act.wait_ge(kt_mm, u + 1)
                if u:
                    act.wait_ge(d_mm, 2 * NS * u)
                act.activation(k_nat[:].rearrange("p a b -> p (a b)"), flat_x[:, 0:NT], ACT.Copy).then_inc(kt_ev, 1)

            def out(pr, h):
                n = 2 * pr + h
                act.wait_ge(o_mm, n + 1)
                if h:
                    act.wait_ge(o_res, n)
                act.activation(o_sb[:], flat_x[:, 0:NT], ACT.Copy).then_inc(o_ev, 1)
                act.wait_ge(o_ev, 2 * n + 1)
                act.activation(o_sq[:], o_sb[:], ACT.Square, scale=DV ** -0.5).then_inc(o_ev, 1)
                act.wait_ge(rms_ok, n + 1)
                act.activation(rms[:], rms[:], ACT.Sqrt).then_inc(rec_ok, 1)
                act.wait_ge(o_res, n + 1)
                act.activation(R.o_hi[:, n], k_nat_f, ACT.Copy).then_inc(o_hi_ok, 1)

            k_nat_f = k_nat[:].rearrange("p a b -> p (a b)")
            for pr in range(PAIRS):
                for dr in range(2):
                    gate(2 * pr + dr)
                    keys(2 * pr + dr)
                for h in range(2):
                    out(pr, h)

        @block.vector
        def _(dve):
            dve.memset(reset[:], 1.0)
            dve.memset(probs[:].rearrange("p a b c d -> p (a b c d)"), 0.0)
            for dr in range(2):
                for n in FIRST[dr]:
                    dve.memset(state[:, dr, n], 0.0)
            dve.memset(ones[:], 1.0).then_inc(made, 1)
            dve.wait_ge(made, 1)
            dve.memset(reset[:].rearrange("p (n c) -> p n c", c=CHUNK)[:, :, 0:1], 0.0).then_inc(made, 1)
            dve.wait_ge(made, 2)
            chain = [0]

            def link(ins):
                chain[0] += 1
                ins.then_inc(dve_in, 1)
                dve.wait_ge(dve_in, chain[0])

            def sums(u, dr):
                cum = cums[:, u % 2]
                dve.wait_ge(soft_ok, u + 1)
                link(dve.scalar_tensor_tensor(z[:], z[:], 0.0, soft[:], ALU.min, ALU.subtract))
                link(dve.tensor_tensor_scan(cum, reset[:], z[:], 0.0, ALU.mult, ALU.add))
                if dr:
                    link(dve.tensor_tensor(z[:], z[:], cum, ALU.subtract))
                    v, last = by_chunk(cum, CHUNK - 1)
                    link(dve.tensor_tensor(z[:].rearrange("p (n c) -> p n c", c=CHUNK),
                                           z[:].rearrange("p (n c) -> p n c", c=CHUNK), last, ALU.add))
                    link(dve.tensor_copy(cum, z[:]))
                v, mid = by_chunk(cum, MID_C[dr])
                v, last = by_chunk(cum, LAST_C[dr])
                if u:
                    dve.wait_ge(s_mm, 2 * u)
                    dve.wait_ge(kt_mm, u)
                dve.tensor_tensor(kk[:].rearrange("p (n c) -> p n c", c=CHUNK), v, mid, ALU.subtract)
                dve.tensor_tensor(k_st[:].rearrange("p (n c) -> p n c", c=CHUNK), last, v,
                                  ALU.subtract).then_inc(cum_ok, 1)

            def unit(u, pr, dr):
                cum = cums[:, u % 2]
                if dr == 0:
                    sums(u, dr)
                dve.wait_ge(e_ok, u + 1)
                if u == 2:
                    dve.wait_ge(o_mm, 2)
                q, k = R.proj[:, M_Q + pr], R.proj[:, M_K + pr]
                dve.scalar_tensor_tensor(qq[:], q, DK ** -0.5, qq[:], ALU.mult, ALU.mult)
                dve.tensor_tensor(kk[:], k, kk[:], ALU.mult)
                dve.scalar_tensor_tensor(q_in[:, dr], q, DK ** -0.5, cum, ALU.mult, ALU.mult)
                dve.tensor_tensor(k_st[:], k, k_st[:], ALU.mult).then_inc(gated, 1)
                for h in range(2):
                    dve.wait_ge(s_mm, 2 * u + h + 1)
                    if u >= 2:
                        dve.wait_ge(o_mm, 2)
                    dve.copy_predicated(probs[:, dr, h], causal[:, dr:dr + 1].bitcast(u32).to_broadcast([P, TT, P]),
                                        flat_x[:, 0:NT].rearrange("p (n c) -> p n c", c=P)).then_inc(s_ev, 1)
                for k, (a, b) in enumerate(STEPS[dr]):
                    if dr == 0 and k == BATCH[dr][1]:
                        sums(u + 1, 1)
                    if k in BATCH[dr]:
                        dve.wait_ge(d_mm, 2 * (NS * u + BATCH[dr][SLOT[dr][k][0] + 1]))
                    if k:
                        dve.wait_ge(st_ok, NS * u + k)
                    at = a * CHUNK + LAST_C[dr]
                    dve.scalar_tensor_tensor(state[:, dr, b], state[:, dr, a], cum[:, at:at + 1],
                                             delta(dr, k), ALU.mult, ALU.add).then_inc(st_ok, 1)

            def out(n):
                dve.wait_ge(o_ev, 2 * n + 1)
                link(dve.scalar_tensor_tensor(o_g[:], o_sb[:], norm_g[:, 0:1], R.proj[:, M_R + n], ALU.mult, ALU.mult))
                dve.wait_ge(ms_mm, n + 1)
                link(dve.tensor_scalar(rms[:], flat_z[:, 0:NT], RMS_EPS, None, ALU.add))
                dve.reciprocal(rms[:], rms[:]).then_inc(rms_ok, 1)
                dve.wait_ge(rec_ok, n + 1)
                if n % 2 == 0:
                    dve.wait_ge(d_mm, 2 * NS * (n + 2))
                dve.tensor_tensor(k_nat_f, o_g[:], rms[:], ALU.mult).then_inc(o_res, 1)
                dve.wait_ge(o_hi_ok, n + 1)
                dve.tensor_tensor(R.o_lo[:, n], k_nat_f, R.o_hi[:, n], ALU.subtract).then_inc(o_lo_ok, 1)
                dve.wait_ge(o_lo_ok, n + 1)

            k_nat_f = k_nat[:].rearrange("p a b -> p (a b)")
            dve.wait_ge(silu_ok, 1)
            dve.wait_ge(consts, 16 * 5)
            for pr in range(PAIRS):
                for dr in range(2):
                    unit(2 * pr + dr, pr, dr)
                for h in range(2):
                    out(2 * pr + h)

        @block.tensor
        def _(pe):
            pe.wait_ge(consts, 16 * 5)
            pe.wait_ge(made, 2)

            def gates(u):
                pr, dr = divmod(u, 2)
                banks = (ps_z, ps_x)[dr]
                if dr:
                    pe.wait_ge(s_ev, 2 * u)
                elif u:
                    pe.wait_ge(st_ok, NS * u)
                if u == 2:
                    pe.wait_ge(rms_ok, 2)
                r0 = AB_ROW * dr
                for b, (t0, n_t) in enumerate(BLOCKS):
                    last = pe.matmul(banks[:, b, 0:n_t], w_a2[r0:r0 + RANK, pr * P:(pr + 1) * P],
                                     R.proj[r0:r0 + RANK, M_LOW, t0:t0 + n_t], start=True, stop=True)
                last.then_inc(z_mm, 1)

            def unit(u, pr, dr):
                pe.wait_ge(gated, u + 1)
                if u:
                    pe.wait_ge(s_ev, 2 * u)
                if u == 2:
                    pe.wait_ge(o_ev, 4)
                for n in range(TT):
                    last = pe.transpose(flat_x[:, n * P:(n + 1) * P], k_st[:, n * P:(n + 1) * P], ident[:])
                last.then_inc(kt_mm, 1)
                for h in range(2):
                    rows = slice(DK * h, DK * (h + 1))
                    if h == 0:
                        pe.wait_ge(kt_ev, u + 1)
                    else:
                        pe.wait_ge(s_ev, 2 * u + 1)
                    for n in range(TT):
                        t = slice(n * P, (n + 1) * P)
                        last = pe.matmul(flat_x[:, t], kk[rows, t], qq[rows, t], start=True, stop=True)
                    last.then_inc(s_mm, 1)
                if dr == 0:
                    gates(u + 1)
                for k, (a, _) in enumerate(STEPS[dr]):
                    batch = SLOT[dr][k][0]
                    if k in BATCH[dr] and batch >= 2:
                        pe.wait_ge(st_ok, NS * u + BATCH[dr][batch - 1])
                    elif k == 0 and u:
                        pe.wait_ge(st_ok, NS * u)
                    for h in range(2):
                        rows = slice(CHUNK * (a % 2), CHUNK * (a % 2 + 1))
                        pe.matmul(delta(dr, k)[DK * h:DK * (h + 1)], k_nat[rows, a // 2, DK * h:DK * (h + 1)],
                                  R.v[rows, a // 2, (2 * pr + h) * DV:(2 * pr + h + 1) * DV],
                                  start=True, stop=True).then_inc(d_mm, 1)

            def out(pr, h):
                n_h = 2 * pr + h
                pe.wait_ge(st_ok, NS * (2 * pr + 2))
                pe.wait_ge(s_ev, 2 * (2 * pr + 2))
                if h:
                    pe.wait_ge(o_ev, 2 * n_h - 1)
                rows = slice(DK * h, DK * (h + 1))
                for n in range(TT):
                    t = slice(n * P, (n + 1) * P)
                    v = R.v[:, n, n_h * DV:(n_h + 1) * DV]
                    pe.matmul(flat_x[:, t], v, probs[:, 0, h, n], start=True, stop=False)
                    more = [(dr, ch) for ch in (2 * n, 2 * n + 1) for dr in range(2) if ch not in FIRST[dr]]
                    last = pe.matmul(flat_x[:, t], v, probs[:, 1, h, n], start=False, stop=not more)
                    for m, (dr, ch) in enumerate(more):
                        tc = slice(ch * CHUNK, (ch + 1) * CHUNK)
                        last = pe.matmul(flat_x[:, tc], state[rows, dr, ch], q_in[rows, dr, tc],
                                         start=False, stop=m == len(more) - 1)
                last.then_inc(o_mm, 1)

            def mean_square(n_h):
                pe.wait_ge(o_ev, 2 * n_h + 2)
                if n_h % 2:
                    pe.wait_ge(rms_ok, n_h)
                for b, (t0, n_t) in enumerate(BLOCKS):
                    last = pe.matmul(ps_z[:, b, 0:n_t], ones[:], o_sq[:, t0:t0 + n_t], start=True, stop=True)
                last.then_inc(ms_mm, 1)

            for pr in range(PAIRS):
                gates(2 * pr)
                for dr in range(2):
                    unit(2 * pr + dr, pr, dr)
                for h in range(2):
                    out(pr, h)
                    mean_square(2 * pr + h)


def fourier(nc, A, R):
    with ExitStack() as c:
        sb = lambda n, s, d: c.enter_context(nc.sbuf_tensor(n, s, d))
        sem = lambda n: R.stack.enter_context(nc.semaphore(n))
        KT = SEQS[0] // P
        f_hi, f_lo = sb("f_f_hi", [P, NT], f16), sb("f_f_lo", [P, NT], f16)
        dft_c = sb("f_dft_c", [P, 2, 2 * GDIM], f16)
        dft_t = sb("f_dft_t", [P, 2, 2, KT, SEQS[0]], f16)
        dft_s = sb("f_dft_s", [P, 2, 2, SEQS[1] // P, SEQS[1]], f16)
        ab = sb("f_ab", [P, 2, 2 * GDIM], f32)
        ab_hi, ab_lo = sb("f_ab_hi", [P, 2, TT, 2 * GDIM], f16), sb("f_ab_lo", [P, 2, TT, 2 * GDIM], f16)
        out = sb("f_out", [P, 2, 512], f32)
        ps_c = c.enter_context(nc.psum_tensor("f_ps_c", [P, 4, 512], f32))
        ps_t = c.enter_context(nc.psum_tensor("f_ps_t", [P, 4, 512], f32))
        tables, f_hi_ok, f_lo_ok, c_mm, c_ev, c_hi, c_lo, t_mm, t_ev, t_hi, t_lo = [sem("f_" + n) for n in
            "tables f_hi_ok f_lo_ok c_mm c_ev c_hi c_lo t_mm t_ev t_hi t_lo".split()]
        time_in = sem("f_time_in")
        BANKS = [(0, 512, 0, KT, dft_t, 0), (512, 512, 0, KT, dft_t, 512), (SEQS[0], SEQS[1], KT, SEQS[1] // P, dft_s, 0)]

        def in_order(channels, time):
            channels(0)
            for g in range(GROUPS):
                if g + 1 < GROUPS:
                    channels(g + 1)
                time(g)
        block = c.enter_context(nc.Block())

        @block.sync
        def _(sp):
            sp.dma_start(dft_c[:], A["dft_c"]).then_inc(tables, 16)
            sp.dma_start(dft_t[:], A["dft_t"]).then_inc(time_in, 16)
            sp.dma_start(dft_s[:], A["dft_s"]).then_inc(time_in, 16)

        @block.scalar
        def _(act):
            def channels(g):
                if g:
                    act.wait_ge(c_mm, TT * g)
                if g >= 2:
                    act.wait_ge(t_mm, NB * (g - 1))
                act.activation(f_hi[:], R.proj[:, M_F + g], ACT.Copy).then_inc(f_hi_ok, 1)
                for t in range(TT):
                    n = TT * g + t
                    act.wait_ge(c_mm, n + 1)
                    if n >= 2:
                        act.wait_ge(c_lo, n - 1)
                    act.activation(ab[:, n % 2], ps_c[:, n % 4, 0:2 * GDIM], ACT.Copy,
                                   scale=GDIM ** -0.5 / WSCALE).then_inc(c_ev, 1)
                    act.wait_ge(c_ev, n + 1)
                    act.activation(ab_hi[:, g % 2, t], ab[:, n % 2], ACT.Copy).then_inc(c_hi, 1)

            def time(g):
                for b, (t0, n_t, *_) in enumerate(BANKS):
                    n = NB * g + b
                    act.wait_ge(t_mm, n + 1)
                    if n >= 2:
                        act.wait_ge(t_lo, n - 1)
                    act.activation(out[:, n % 2, 0:n_t], ps_t[:, n % 4, 0:n_t], ACT.Copy,
                                   scale=(SEQS[0] if t0 < SEQS[0] else SEQS[1]) ** -0.5 / WSCALE).then_inc(t_ev, 1)
                    act.wait_ge(t_ev, n + 1)
                    act.activation(R.f_hi[:, g, t0:t0 + n_t], out[:, n % 2, 0:n_t], ACT.Copy).then_inc(t_hi, 1)
            in_order(channels, time)

        @block.vector
        def _(dve):
            def channels(g):
                dve.wait_ge(f_hi_ok, g + 1)
                dve.tensor_tensor(f_lo[:], R.proj[:, M_F + g], f_hi[:], ALU.subtract).then_inc(f_lo_ok, 1)
                for t in range(TT):
                    n = TT * g + t
                    dve.wait_ge(c_hi, n + 1)
                    dve.tensor_tensor(ab_lo[:, g % 2, t], ab[:, n % 2], ab_hi[:, g % 2, t], ALU.subtract).then_inc(c_lo, 1)

            def time(g):
                for b, (t0, n_t, *_) in enumerate(BANKS):
                    n = NB * g + b
                    dve.wait_ge(t_hi, n + 1)
                    dve.tensor_tensor(R.f_lo[:, g, t0:t0 + n_t], out[:, n % 2, 0:n_t], R.f_hi[:, g, t0:t0 + n_t],
                                      ALU.subtract).then_inc(t_lo, 1)
            in_order(channels, time)

        @block.tensor
        def _(pe):
            pe.wait_ge(tables, 16)
            def channels(g):
                pe.wait_ge(f_lo_ok, g + 1)
                for t in range(TT):
                    n = TT * g + t
                    if n >= 4:
                        pe.wait_ge(c_ev, n - 3)
                    cols = slice(t * P, (t + 1) * P)
                    hi_lo(pe, ps_c[:, n % 4, 0:2 * GDIM], f_hi[:, cols], f_lo[:, cols], dft_c[:, 0], dft_c[:, 1],
                          True, True).then_inc(c_mm, 1)

            def time(g):
                pe.wait_ge(c_lo, TT * (g + 1))
                pe.wait_ge(time_in, 32)
                for b, (t0, n_t, k0, n_k, table, col) in enumerate(BANKS):
                    n = NB * g + b
                    if n >= 4:
                        pe.wait_ge(t_ev, n - 3)
                    for k in range(n_k):
                        for s in range(2):
                            ch = slice(s * GDIM, (s + 1) * GDIM)
                            last = hi_lo(pe, ps_t[:, n % 4, 0:n_t], ab_hi[:, g % 2, k0 + k, ch],
                                         ab_lo[:, g % 2, k0 + k, ch], table[:, s, 0, k, col:col + n_t],
                                         table[:, s, 1, k, col:col + n_t], k == 0 and s == 0, k == n_k - 1 and s == 1)
                    last.then_inc(t_mm, 1)
            in_order(channels, time)


def merge(nc, A, R):
    with ExitStack() as c:
        sb = lambda n, s, d: c.enter_context(nc.sbuf_tensor(n, s, d))
        sem = lambda n: R.stack.enter_context(nc.semaphore(n))
        x_hi, x_lo = sb("m_x_hi", [P, KO, NT], f16), sb("m_x_lo", [P, KO, NT], f16)
        KW = 2 * KO + 2 * HEADS
        w_st = sb("m_w_st", [P, 2, KW * P], f32)
        w_hi, w_lo = sb("m_w_hi", [P, 2, KW * P], f16), sb("m_w_lo", [P, 2, KW * P], f16)
        b_mg = sb("m_b_mg", [P, 2, KO], f32)
        s1, s2 = sb("m_s1", [P, 2, 512], f32), sb("m_s2", [P, 2, 512], f32)
        t1, t2, mg = sb("m_t1", [P, 512], f32), sb("m_t2", [P, 512], f32), sb("m_mg", [P, 2, 512], f32)
        ps = c.enter_context(nc.psum_tensor("m_ps", [P, 2, 4, 512], f32))
        x_in, bias_in = sem("m_x_in"), sem("m_bias_in")
        w_in = [sem("m_w_in0"), sem("m_w_in1")]
        w_hi_ok, w_lo_ok, mm, sig, prod, mg_ok, mg_hi, mg_lo = [sem("m_" + n) for n in
            "w_hi_ok w_lo_ok mm sig prod mg_ok mg_hi mg_lo".split()]
        block = c.enter_context(nc.Block())

        @block.sync
        def _(sp):
            sp.dma_start(w_st[:, 0], A["w_merge"][0]).then_inc(w_in[0], 16)
            sp.dma_start(x_hi[:], R.x_hi_dram).then_inc(x_in, 16)
            sp.dma_start(x_lo[:], R.x_lo_dram).then_inc(x_in, 16)
            sp.dma_start(b_mg[:], A["b_mg"]).then_inc(bias_in, 16)
            sp.dma_start(w_st[:, 1], A["w_merge"][1]).then_inc(w_in[1], 16)
            with sp.Fori(1, KO // 2) as i:
                for q in range(2):
                    sp.wait_ge(w_lo_ok, 2 * i + q - 1)
                    sp.dma_start(w_st[:, q], A["w_merge"][2 * i + q]).then_inc(w_in[q], 16)

        def split_hi(act, m, q, nth):
            act.wait_ge(w_in[q], nth)
            if not isinstance(m, int) or m >= 2:
                act.wait_ge(mm, NB * (m - 1))
            act.activation(w_hi[:, q], w_st[:, q], ACT.Copy, scale=WSCALE).then_inc(w_hi_ok, 1)

        @block.scalar
        def _(act):
            def steps(m, q):
                for b, (t0, n_t) in enumerate(BLOCKS):
                    n, s = NB * m + b, (NB * q + b) % 2
                    act.wait_ge(mm, n + 1)
                    if not (isinstance(n, int) and n < 2):
                        wait_apart(act, mg_ok, n - 1)
                    act.activation(s1[:, s, 0:n_t], ps[:, s, 0, 0:n_t], ACT.Sigmoid, scale=1 / WSCALE,
                                   bias=b_mg[:, 0, m:m + 1] if isinstance(m, int) else b_mg[:, 0, bass.ds(m, 1)])
                    act.activation(s2[:, s, 0:n_t], ps[:, s, 1, 0:n_t], ACT.Sigmoid, scale=1 / WSCALE,
                                   bias=b_mg[:, 1, m:m + 1] if isinstance(m, int) else b_mg[:, 1, bass.ds(m, 1)]
                                   ).then_inc(sig, 1)
                    wait_apart(act, mg_ok, n + 1)
                    act.activation(R.m_hi[:, m, t0:t0 + n_t], mg[:, s, 0:n_t], ACT.Copy).then_inc(mg_hi, 1)
            act.wait_ge(bias_in, 16)
            split_hi(act, 0, 0, 16)
            split_hi(act, 1, 1, 16)
            steps(0, 0)
            with act.Fori(1, KO // 2) as i:
                split_hi(act, 2 * i, 0, 16 * i + 16)
                steps(2 * i - 1, 1)
                split_hi(act, 2 * i + 1, 1, 16 * i + 16)
                steps(2 * i, 0)
            steps(KO - 1, 1)

        @block.vector
        def _(dve):
            def split_lo(m, q):
                dve.wait_ge(w_hi_ok, m + 1)
                dve.scalar_tensor_tensor(w_lo[:, q], w_st[:, q], WSCALE, w_hi[:, q], ALU.mult,
                                         ALU.subtract).then_inc(w_lo_ok, 1)

            def steps(m, q):
                for b, (t0, n_t) in enumerate(BLOCKS):
                    n, s = NB * m + b, (NB * q + b) % 2
                    dve.wait_ge(sig, n + 1)
                    dve.scalar_tensor_tensor(t1[:, 0:n_t], ps[:, s, 2, 0:n_t], 1 / WSCALE, s1[:, s, 0:n_t],
                                             ALU.mult, ALU.mult)
                    dve.scalar_tensor_tensor(t2[:, 0:n_t], ps[:, s, 3, 0:n_t], 1 / WSCALE, s2[:, s, 0:n_t],
                                             ALU.mult, ALU.mult).then_inc(prod, 1)
                    dve.wait_ge(prod, n + 1)
                    dve.tensor_tensor(mg[:, s, 0:n_t], t1[:, 0:n_t], t2[:, 0:n_t], ALU.add).then_inc(mg_ok, 1)
                    dve.wait_ge(mg_hi, n + 1)
                    dve.tensor_tensor(R.m_lo[:, m, t0:t0 + n_t], mg[:, s, 0:n_t], R.m_hi[:, m, t0:t0 + n_t],
                                      ALU.subtract).then_inc(mg_lo, 1)
            split_lo(0, 0)
            split_lo(1, 1)
            steps(0, 0)
            with dve.Fori(1, KO // 2) as i:
                split_lo(2 * i, 0)
                steps(2 * i - 1, 1)
                split_lo(2 * i + 1, 1)
                steps(2 * i, 0)
            steps(KO - 1, 1)

        @block.tensor
        def _(pe):
            def tile(m, q, peeled):
                pe.wait_ge(w_lo_ok, m + 1)
                for b, (t0, n_t) in enumerate(BLOCKS):
                    n, s = NB * m + b, (NB * q + b) % 2
                    if not (isinstance(n, int) and n < 2):
                        pe.wait_ge(mg_ok, n - 1)
                    t = slice(t0, t0 + n_t)
                    at = 0
                    for o, (hi, lo, n_k) in enumerate(((x_hi, x_lo, KO), (x_hi, x_lo, KO),
                                                       (R.o_hi, R.o_lo, HEADS), (R.f_hi, R.f_lo, GROUPS))):
                        for k in range(n_k):
                            w = slice(at * P, (at + 1) * P)
                            last = hi_lo(pe, ps[:, s, o, 0:n_t], w_hi[:, q, w], w_lo[:, q, w], hi[:, k, t], lo[:, k, t],
                                         k == 0, k == n_k - 1)
                            at += 1
                    last.then_inc(mm, 1)
            pe.wait_ge(x_in, 32)
            tile(0, 0, True)
            tile(1, 1, True)
            with pe.Fori(1, KO // 2) as i:
                tile(2 * i, 0, False)
                tile(2 * i + 1, 1, False)


def layer_norm_steps(dve, y, stats, mv, gain, shift, link, rms_ready, rms_taken, n):
    for half in range(2):
        last = dve.bn_stats(stats[:, half], y[:, half * 512:(half + 1) * 512])
    link(last)
    link(dve.bn_aggr(mv[:, 0:2], stats[:].rearrange("p a b -> p (a b)")))
    dve.tensor_scalar(mv[:, 2:3], mv[:, 1:2], LN_EPS, None, ALU.add).then_inc(rms_ready, 1)
    dve.wait_ge(rms_taken, n + 1)
    link(dve.reciprocal(mv[:, 3:4], mv[:, 2:3]))
    link(dve.tensor_scalar(y, y, mv[:, 0:1], mv[:, 3:4], ALU.subtract, ALU.mult))
    link(dve.tensor_tensor(y, y, gain, ALU.mult))
    return dve.tensor_tensor(y, y, shift, ALU.add)


def linker(dve, sem):
    chain = [0]

    def link(ins):
        chain[0] += 1
        ins.then_inc(sem, 1)
        dve.wait_ge(sem, chain[0])
    return link


def mix_norm(nc, A, R):
    with ExitStack() as c:
        sb = lambda n, s, d: c.enter_context(nc.sbuf_tensor(n, s, d))
        sem = lambda n: R.stack.enter_context(nc.semaphore(n))
        w_st = sb("o_w_st", [P, 2, D], f32)
        w_hi, w_lo = sb("o_w_hi", [P, KO, D], f16), sb("o_w_lo", [P, KO, D], f16)
        x = sb("o_x", [P, 2, D], f32)
        y = sb("o_y", [P, 2, D], f32)
        gain, shift = sb("o_gain", [P, D], f32), sb("o_shift", [P, D], f32)
        ident = sb("o_ident", [P, P], f32)
        stats, mv = sb("o_stats", [P, 2, 6], f32), sb("o_mv", [P, 4], f32)
        ps = c.enter_context(nc.psum_tensor("o_ps", [P, 2, D], f32))
        ps_t = c.enter_context(nc.psum_tensor("o_ps_t", [P, 2, KO, P], f32))
        w_in = [sem("o_w_in0"), sem("o_w_in1")]
        x_in = [sem("o_x_in0"), sem("o_x_in1")]
        consts, w_hi_ok, w_lo_ok, mm, ax_ok, y_ok, v_ok, sq_ok, h_ok, t_mm, acc_ok, hi_ok, lo_ok, dve_in = [
            sem("o_" + n) for n in "consts w_hi_ok w_lo_ok mm ax_ok y_ok v_ok sq_ok h_ok t_mm acc_ok hi_ok lo_ok dve_in".split()]
        block = c.enter_context(nc.Block())

        @block.sync
        def _(sp):
            for k in range(KO):
                if k >= 2:
                    sp.wait_ge(w_lo_ok, k - 1)
                sp.dma_start(w_st[:, k % 2], A["w_o"][k]).then_inc(w_in[k % 2], 16)
                if k == 1:
                    sp.dma_start(gain[:], A["ln1_g"].to_broadcast([P, D])).then_inc(consts, 16)
                    sp.dma_start(shift[:], A["ln1_b"].to_broadcast([P, D])).then_inc(consts, 16)
                    sp.dma_start(ident[:], A["ident"]).then_inc(consts, 16)
                    for t in range(2):
                        sp.dma_start(x[:, t], A["x"][t]).then_inc(x_in[t], 16)
            for t in range(2, TT):
                sp.wait_ge(y_ok, t - 1)
                sp.dma_start(x[:, t % 2], A["x"][t]).then_inc(x_in[t % 2], 16)

        @block.scalar
        def _(act):
            for k in range(KO):
                act.wait_ge(w_in[k % 2], 16 * (k // 2 + 1))
                act.activation(w_hi[:, k], w_st[:, k % 2], ACT.Copy, scale=WSCALE).then_inc(w_hi_ok, 1)

            def scaled_x(t):
                act.wait_ge(x_in[t % 2], 16 * (t // 2 + 1))
                act.activation(x[:, t % 2], x[:, t % 2], ACT.Copy, scale=ALPHA).then_inc(ax_ok, 1)
            scaled_x(0)
            for t in range(TT):
                act.wait_ge(v_ok, t + 1)
                act.activation(mv[:, 2:3], mv[:, 2:3], ACT.Sqrt).then_inc(sq_ok, 1)
                if t + 1 < TT:
                    scaled_x(t + 1)
                act.wait_ge(h_ok, t + 1)
                if t >= DT:
                    act.activation(R.h_nat[:, t - DT], y[:, t % 2], ACT.Copy)
                act.activation(R.acc[:, t], y[:, t % 2], ACT.Copy, scale=ALPHA).then_inc(acc_ok, 1)
                act.wait_ge(t_mm, t + 1)
                act.activation(R.h_hi[:, :, t * P:(t + 1) * P], ps_t[:, t % 2], ACT.Copy).then_inc(hi_ok, 1)

        @block.vector
        def _(dve):
            for k in range(KO):
                dve.wait_ge(w_hi_ok, k + 1)
                dve.scalar_tensor_tensor(w_lo[:, k], w_st[:, k % 2], WSCALE, w_hi[:, k], ALU.mult,
                                         ALU.subtract).then_inc(w_lo_ok, 1)
            link = linker(dve, dve_in)
            dve.wait_ge(consts, 48)

            def low_part(t):
                dve.wait_ge(hi_ok, t + 1)
                dve.tensor_tensor(R.h_lo[:, :, t * P:(t + 1) * P], ps_t[:, t % 2], R.h_hi[:, :, t * P:(t + 1) * P],
                                  ALU.subtract).then_inc(lo_ok, 1)
            for t in range(TT):
                dve.wait_ge(mm, t + 1)
                dve.wait_ge(ax_ok, t + 1)
                if t >= 2:
                    dve.wait_ge(acc_ok, t - 1)
                    dve.wait_ge(t_mm, t - 1)
                dve.scalar_tensor_tensor(y[:, t % 2], ps[:, t % 2], 1 / WSCALE, x[:, t % 2], ALU.mult,
                                         ALU.add).then_inc(y_ok, 1)
                dve.wait_ge(y_ok, t + 1)
                layer_norm_steps(dve, y[:, t % 2], stats, mv, gain[:], shift[:], link, v_ok, sq_ok, t).then_inc(h_ok, 1)
                if t:
                    low_part(t - 1)
            low_part(TT - 1)

        @block.tensor
        def _(pe):
            pe.wait_ge(consts, 48)
            pe.wait_ge(w_lo_ok, KO)

            def transposes(t):
                pe.wait_ge(h_ok, t + 1)
                if t >= 2:
                    pe.wait_ge(lo_ok, t - 1)
                for k in range(KO):
                    last = pe.transpose(ps_t[:, t % 2, k], y[:, t % 2, k * P:(k + 1) * P], ident[:])
                last.then_inc(t_mm, 1)
            for t in range(TT):
                if t >= 2:
                    pe.wait_ge(y_ok, t - 1)
                for k in range(KO):
                    lhs = R.m_hi[:, k, t * P:(t + 1) * P], R.m_lo[:, k, t * P:(t + 1) * P]
                    for half in range(2):
                        n = slice(half * 512, (half + 1) * 512)
                        last = hi_lo(pe, ps[:, t % 2, n], *lhs, w_hi[:, k, n], w_lo[:, k, n], k == 0, k == KO - 1)
                last.then_inc(mm, 1)
                if t:
                    transposes(t - 1)
            transposes(TT - 1)


def best_keys(nc, A, R):
    with ExitStack() as c:
        sb = lambda n, s, d: c.enter_context(nc.sbuf_tensor(n, s, d))
        sem = lambda n: R.stack.enter_context(nc.semaphore(n))
        KW = KO + 1
        w_st = sb("k_w_st", [P, 2, KW * P], f32)
        w_hi, w_lo = sb("k_w_hi", [P, 2, KO * P], f16), sb("k_w_lo", [P, 2, KO * P], f16)
        k_hi, k_lo = sb("k_k_hi", [P, 2, P], f16), sb("k_k_lo", [P, 2, P], f16)
        q = sb("k_q", [P, 2, NT], f32)
        q_hi, q_lo = sb("k_q_hi", [P, 2, NT], f16), sb("k_q_lo", [P, 2, NT], f16)
        sc = sb("k_sc", [P, 2, TT, P], f32)
        rest = sb("k_rest", [P, TT, P], f32)
        val, idx = sb("k_val", [P, TT, TOPK], f32), sb("k_idx", [P, TT, TOPK], u32)
        ps = c.enter_context(nc.psum_tensor("k_ps", [P, 3, 512], f32))
        ps_s = c.enter_context(nc.psum_tensor("k_ps_s", [P, 3, 512], f32))
        flat_s = ps_s[:].rearrange("p a b -> p (a b)")
        w_in = [sem("k_w_in0"), sem("k_w_in1")]
        k_hi_ok, k_lo_ok = sem("k_k_hi_ok"), sem("k_k_lo_ok")
        w_hi_ok, w_lo_ok, q_mm, q_ev, q_hi_ok, q_lo_ok, s_mm, s_ev, v_ok, i_ok, kept = [sem("k_" + n) for n in
            "w_hi_ok w_lo_ok q_mm q_ev q_hi_ok q_lo_ok s_mm s_ev v_ok i_ok kept".split()]
        block = c.enter_context(nc.Block())

        @block.sync
        def _(sp):
            for m in range(2):
                sp.dma_start(w_st[:, m], A["w_route"][m]).then_inc(w_in[m], 16)
            with sp.Fori(1, HP // 2) as i:
                for s in range(2):
                    sp.wait_ge(w_lo_ok, 2 * i + s - 1)
                    sp.wait_ge(k_lo_ok, 2 * i + s - 1)
                    sp.dma_start(w_st[:, s], A["w_route"][2 * i + s]).then_inc(w_in[s], 16)

        @block.scalar
        def _(act):
            def split_w(m, s, nth, first=False):
                act.wait_ge(w_in[s], nth)
                if not first:
                    act.wait_ge(q_mm, NB * (m - 1))
                act.activation(w_hi[:, s], w_st[:, s, 0:KO * P], ACT.Copy, scale=WSCALE).then_inc(w_hi_ok, 1)

            def split_k(m, s, nth, first=False):
                act.wait_ge(w_in[s], nth)
                if not first:
                    act.wait_ge(s_mm, m - 1)
                act.activation(k_hi[:, s], w_st[:, s, KO * P:], ACT.Copy, scale=WSCALE).then_inc(k_hi_ok, 1)

            def queries(m, s, first=False):
                for b, (t0, n_t) in enumerate(BLOCKS):
                    act.wait_ge(q_mm, NB * m + b + 1)
                    if not first:
                        act.wait_ge(s_mm, m - 1)
                        act.wait_ge(q_lo_ok, m - 1)
                    last = act.activation(q[:, s, t0:t0 + n_t], ps[:, b, 0:n_t], ACT.Copy, scale=1 / WSCALE)
                    last.then_inc(q_ev, 1)
                act.wait_ge(q_ev, NB * m + NB)
                act.activation(q_hi[:, s], q[:, s], ACT.Copy).then_inc(q_hi_ok, 1)

            def scores(m, s, first=False):
                act.wait_ge(s_mm, m + 1)
                if not first:
                    act.wait_ge(kept, m)
                act.activation(sc[:, s].rearrange("p a b -> p (a b)"), flat_s[:, 0:NT], ACT.Copy,
                               scale=1 / WSCALE).then_inc(s_ev, 1)
            split_w(0, 0, 16, True)
            split_w(1, 1, 16, True)
            split_k(0, 0, 16, True)
            queries(0, 0, True)
            split_w(2, 0, 32)
            split_k(1, 1, 16, True)
            queries(1, 1, True)
            split_w(3, 1, 32)
            split_k(2, 0, 32)
            scores(0, 0, True)
            with act.Fori(1, HP // 2 - 1) as i:
                queries(2 * i, 0)
                split_w(2 * i + 2, 0, 16 * i + 32)
                split_k(2 * i + 1, 1, 16 * i + 16)
                scores(2 * i - 1, 1)
                queries(2 * i + 1, 1)
                split_w(2 * i + 3, 1, 16 * i + 32)
                split_k(2 * i + 2, 0, 16 * i + 32)
                scores(2 * i, 0)
            queries(HP - 2, 0)
            split_k(HP - 1, 1, 16 * (HP // 2))
            scores(HP - 3, 1)
            queries(HP - 1, 1)
            scores(HP - 2, 0)
            scores(HP - 1, 1)

        @block.vector
        def _(dve):
            def split_w(m, s):
                dve.wait_ge(w_hi_ok, m + 1)
                dve.scalar_tensor_tensor(w_lo[:, s], w_st[:, s, 0:KO * P], WSCALE, w_hi[:, s], ALU.mult,
                                         ALU.subtract).then_inc(w_lo_ok, 1)

            def split_k(m, s):
                dve.wait_ge(k_hi_ok, m + 1)
                dve.scalar_tensor_tensor(k_lo[:, s], w_st[:, s, KO * P:], WSCALE, k_hi[:, s], ALU.mult,
                                         ALU.subtract).then_inc(k_lo_ok, 1)

            def queries(m, s):
                dve.wait_ge(q_hi_ok, m + 1)
                dve.tensor_tensor(q_lo[:, s], q[:, s], q_hi[:, s], ALU.subtract).then_inc(q_lo_ok, 1)

            def top(m, s):
                wait_apart(dve, s_ev, m + 1)
                wait_apart(dve, kept, m + 1)
                for t in range(TT):
                    last = dve.max(val[:, t, 0:8], sc[:, s, t])
                last.then_inc(v_ok, 1)
                wait_apart(dve, v_ok, 3 * m + 1)
                for t in range(TT):
                    dve.max_index(idx[:, t, 0:8], val[:, t, 0:8], sc[:, s, t])
                    last = dve.match_replace(rest[:, t], val[:, t, 0:8], sc[:, s, t], LOWEST)
                last.then_inc(v_ok, 1)
                wait_apart(dve, v_ok, 3 * m + 2)
                for t in range(TT):
                    last = dve.max(val[:, t, 8:16], rest[:, t])
                last.then_inc(v_ok, 1)
                wait_apart(dve, v_ok, 3 * m + 3)
                for t in range(TT):
                    last = dve.max_index(idx[:, t, 8:16], val[:, t, 8:16], rest[:, t])
                last.then_inc(i_ok, 1)
                dve.wait_ge(i_ok, m + 1)
                dve.tensor_copy(R.top_v[:, m], val[:])
                dve.tensor_copy(R.top_i[:, m], idx[:]).then_inc(kept, 1)
            dve.sem_inc(kept, 1)
            split_w(0, 0)
            split_w(1, 1)
            split_k(0, 0)
            queries(0, 0)
            split_w(2, 0)
            split_k(1, 1)
            queries(1, 1)
            split_w(3, 1)
            split_k(2, 0)
            top(0, 0)
            with dve.Fori(1, HP // 2 - 1) as i:
                queries(2 * i, 0)
                split_w(2 * i + 2, 0)
                split_k(2 * i + 1, 1)
                top(2 * i - 1, 1)
                queries(2 * i + 1, 1)
                split_w(2 * i + 3, 1)
                split_k(2 * i + 2, 0)
                top(2 * i, 0)
            queries(HP - 2, 0)
            split_k(HP - 1, 1)
            top(HP - 3, 1)
            queries(HP - 1, 1)
            top(HP - 2, 0)
            top(HP - 1, 1)

        @block.tensor
        def _(pe):
            def project_half(m, s, first=False):
                pe.wait_ge(w_lo_ok, m + 1)
                for b, (t0, n_t) in enumerate(BLOCKS):
                    if not first:
                        pe.wait_ge(q_ev, NB * m + b - 2)
                    t = slice(t0, t0 + n_t)
                    for k in range(KO):
                        w = slice(k * P, (k + 1) * P)
                        last = hi_lo(pe, ps[:, b, 0:n_t], w_hi[:, s, w], w_lo[:, s, w], R.h_hi[:, k, t],
                                     R.h_lo[:, k, t], k == 0, k == KO - 1)
                    last.then_inc(q_mm, 1)

            def score(m, s, first=False):
                pe.wait_ge(q_lo_ok, m + 1)
                if not first:
                    pe.wait_ge(s_ev, m)
                pe.wait_ge(k_lo_ok, m + 1)
                for t in range(TT):
                    cols = slice(t * P, (t + 1) * P)
                    last = hi_lo(pe, flat_s[:, cols], q_hi[:, s, cols], q_lo[:, s, cols], k_hi[:, s],
                                 k_lo[:, s], True, True)
                last.then_inc(s_mm, 1)
            project_half(0, 0, True)
            project_half(1, 1)
            score(0, 0, True)
            with pe.Fori(1, HP // 2) as i:
                project_half(2 * i, 0)
                score(2 * i - 1, 1)
                project_half(2 * i + 1, 1)
                score(2 * i, 0)
            score(HP - 1, 1)


def best_pairs(nc, A, R):
    with ExitStack() as c:
        sb = lambda n, s, d: c.enter_context(nc.sbuf_tensor(n, s, d))
        sem = lambda n: R.stack.enter_context(nc.semaphore(n))
        NC = TOPK * TOPK
        KP = PLE // P
        KW = KO + KP
        ident = sb("b_ident", [P, P], f32)
        steps = sb("b_steps", [P, TOPK], f32)
        cand = sb("b_cand", [P, PH, TOPK, TOPK], f32)
        best = sb("b_best", [P, PH, TOPK], f32)
        pos = sb("b_pos", [P, PH, TOPK], u32)
        part = sb("b_part", [P, 2, P], u32)
        place = pos[:].rearrange("p h k -> p (h k)").bitcast(f16)
        pair = sb("b_hits_iota", [P, 2, TOPK, 2 * P], f16)
        hits, iota = pair[:, 0], pair[:, 1]
        gij = sb("b_gij", [P, 3, P], f32)
        ex = sb("b_ex", [P, PH, TOPK], f32)
        den = sb("b_den", [P, PH, 2], f32)
        w_hi, w_lo = sb("b_w_hi", [P, KW, D], f16), sb("b_w_lo", [P, KW, D], f16)
        p_hi, p_lo = sb("b_p_hi", [P, KP, NT], f16), sb("b_p_lo", [P, KP, NT], f16)
        s_g = sb("b_s_g", [P, D], f32)
        w_st = cand[:].rearrange("p h a b -> p (h a b)").rearrange("p (s d) -> p s d", d=D)
        p_st = pair[:].rearrange("p s a n -> p (s a n)").bitcast(f32)[:, 0:KP * NT].rearrange("p (k t) -> p k t", k=KP)
        ps = c.enter_context(nc.psum_tensor("b_ps", [P, 2, 512], f32))
        ps_g = c.enter_context(nc.psum_tensor("b_ps_g", [P, 2, D], f32))
        ps_p = c.enter_context(nc.psum_tensor("b_ps_p", [P, D], f32))
        consts, dve_in, dif_ok, exp_ok, gij_ok, t_mm, t_ev, g_lo_ok = [sem("b_" + n) for n in
            "consts dve_in dif_ok exp_ok gij_ok t_mm t_ev g_lo_ok".split()]
        iota_ok, hits_ok, picked_ok = sem("b_iota_ok"), sem("b_hits_ok"), sem("b_picked_ok")
        w_in = [sem("b_w_in0"), sem("b_w_in1")]
        p_in, w_hi_ok, w_lo_ok, p_hi_ok, p_lo_ok, e_mm, sig, prod, added = [sem("b_" + n) for n in
            "p_in w_hi_ok w_lo_ok p_hi_ok p_lo_ok e_mm sig prod added".split()]
        LINKS = 14
        LOOPED = DT // 2
        block = c.enter_context(nc.Block())

        def tiles(eng, tile):
            tile(0, 0, True, False)
            tile(1, 1, True, False)
            with eng.Fori(1, LOOPED) as i:
                tile(2 * i, 0, False, False)
                tile(2 * i + 1, 1, False, False)
            for t in range(2 * LOOPED, TT):
                tile(t, t % 2, False, t >= DT)

        @block.sync
        def _(sp):
            for k in range(KW):
                if k >= 2:
                    sp.wait_ge(w_lo_ok, k - 1)
                sp.dma_start(w_st[:, k % 2], A["w_ple"][k]).then_inc(w_in[k % 2], 16)
                if k == 1:
                    sp.dma_start(p_st, A["p_t"]).then_inc(p_in, 16)
                    sp.dma_start(ident[:], A["ident"]).then_inc(consts, 16)
                    sp.dma_start(steps[:], A["iota"][0:TOPK].rearrange("(a n) -> a n", a=1).to_broadcast([P, TOPK])
                                 ).then_inc(consts, 16)

        @block.scalar
        def _(act):
            for k in range(KW):
                act.wait_ge(w_in[k % 2], 16 * (k // 2 + 1))
                act.activation(w_hi[:, k], w_st[:, k % 2], ACT.Copy, scale=WSCALE).then_inc(w_hi_ok, 1)
                if k == 1:
                    act.wait_ge(p_in, 16)
                    act.activation(p_hi[:], p_st, ACT.Copy).then_inc(p_hi_ok, 1)

            def tile(t, s, peeled, _):
                wait_apart(act, e_mm, t + 1)
                if isinstance(t, int) and t == 0:
                    pass
                else:
                    wait_apart(act, added, t)
                act.activation(s_g[:], ps_g[:, s], ACT.Sigmoid, scale=1 / WSCALE).then_inc(sig, 1)
                act.wait_ge(dif_ok, t + 1)
                act.activation(ex[:], ex[:], ACT.Exp).then_inc(exp_ok, 1)
                wait_apart(act, t_mm, t + 1)
                act.activation(R.g_hi[:, bass.ds(t * P, P)], ps[:, s, 0:P], ACT.Copy, scale=GSCALE)
                act.activation(R.ij[:, :, bass.ds(t * P, P)], ps[:, s, P:3 * P].rearrange("p (a b) -> p a b", a=2),
                               ACT.Copy).then_inc(t_ev, 1)
            tiles(act, tile)

        def pick(eng, half, t):
            names = R.top_i[:, half::2, t].rearrange("p h (a b) -> p h a b", b=1).to_broadcast([P, PH, TOPK, TOPK])
            picked = hits[:, :, half * P:(half + 1) * P].rearrange("p a (h k) -> p h a k", h=PH)
            return eng.tensor_tensor(picked, picked, names, ALU.mult)

        @block.gpsimd
        def _(pool):
            def tile(t, s, peeled, _):
                wait_apart(pool, hits_ok, t + 1)
                pick(pool, 1, t).then_inc(picked_ok, 1)
            tiles(pool, tile)

        @block.vector
        def _(dve):
            for k in range(KW):
                dve.wait_ge(w_hi_ok, k + 1)
                dve.scalar_tensor_tensor(w_lo[:, k], w_st[:, k % 2], WSCALE, w_hi[:, k], ALU.mult,
                                         ALU.subtract).then_inc(w_lo_ok, 1)
                if k == 1:
                    dve.wait_ge(p_hi_ok, 1)
                    dve.tensor_tensor(p_lo[:], p_st, p_hi[:], ALU.subtract).then_inc(p_lo_ok, 1)
            dve.wait_ge(w_lo_ok, KW)
            dve.wait_ge(p_lo_ok, 1)
            dve.wait_ge(consts, 32)
            dve.tensor_copy(iota, steps[:].rearrange("p (a n) -> p a n", n=1).to_broadcast([P, TOPK, 2 * P])
                            ).then_inc(iota_ok, 1)
            dve.wait_ge(iota_ok, 1)

            def tile(t, s, peeled, fetched):
                count = [0]

                def link(ins):
                    count[0] += 1
                    ins.then_inc(dve_in, 1)
                    wait_apart(dve, dve_in, LINKS * t + count[0])

                if isinstance(t, int) and t == 0:
                    pass
                else:
                    g_low(t - 1, 1 - s)
                first = R.top_v[:, 0::2, t].rearrange("p h (a b) -> p h a b", b=1).to_broadcast([P, PH, TOPK, TOPK])
                second = R.top_v[:, 1::2, t].rearrange("p h (a b) -> p h a b", a=1).to_broadcast([P, PH, TOPK, TOPK])
                link(dve.tensor_tensor(cand[:], first, second, ALU.add))
                rows = [cand[:, h].rearrange("p a b -> p (a b)") for h in range(PH)]
                for h in range(PH):
                    last = dve.max(best[:, h, 0:8], rows[h])
                link(last)
                for h in range(PH):
                    last = dve.max_index(pos[:, h, 0:8], best[:, h, 0:8], rows[h])
                link(last)
                for h in range(PH):
                    last = dve.match_replace(rows[h], best[:, h, 0:8], rows[h], LOWEST)
                link(last)
                for h in range(PH):
                    last = dve.max(best[:, h, 8:16], rows[h])
                link(last)
                for h in range(PH):
                    last = dve.max_index(pos[:, h, 8:16], best[:, h, 8:16], rows[h])
                link(last)
                dve.tensor_tensor(ex[:], best[:], best[:, :, 0:1].to_broadcast([P, PH, TOPK]),
                                  ALU.subtract).then_inc(dif_ok, 1)
                flat = pos[:].rearrange("p h k -> p (h k)")
                dve.tensor_scalar(part[:, 0], flat, 4, None, ALU.logical_shift_right)
                link(dve.tensor_scalar(part[:, 1], flat, TOPK - 1, None, ALU.bitwise_and))
                link(dve.tensor_copy(place, part[:].rearrange("p h n -> p (h n)")))
                chosen = place.rearrange("p (a n) -> p a n", a=1).to_broadcast([P, TOPK, 2 * P])
                dve.tensor_tensor(hits, iota, chosen, ALU.is_equal).then_inc(hits_ok, 1)
                wait_apart(dve, hits_ok, t + 1)
                if not (isinstance(t, int) and t == 0):
                    wait_apart(dve, t_mm, t)
                link(pick(dve, 0, t))
                link(dve.tensor_reduce(gij[:, 1], hits[:, :, 0:P].rearrange("p a n -> p n a"), AX.X, ALU.add))
                wait_apart(dve, sig, t + 1)
                dve.scalar_tensor_tensor(s_g[:], ps_p[:], 1 / WSCALE, s_g[:], ALU.mult, ALU.mult).then_inc(prod, 1)
                wait_apart(dve, prod, t + 1)
                dve.tensor_tensor(R.acc[:, t], R.acc[:, t], s_g[:], ALU.add).then_inc(added, 1)
                wait_apart(dve, exp_ok, t + 1)
                link(dve.tensor_reduce(den[:, :, 0:1], ex[:], AX.X, ALU.add))
                link(dve.reciprocal(den[:, :, 1:2], den[:, :, 0:1]))
                wait_apart(dve, picked_ok, t + 1)
                link(dve.tensor_reduce(gij[:, 2], hits[:, :, P:2 * P].rearrange("p a n -> p n a"), AX.X, ALU.add))
                link(dve.tensor_tensor(gij[:, 0].rearrange("p (h k) -> p h k", h=PH), ex[:],
                                       den[:, :, 1:2].to_broadcast([P, PH, TOPK]), ALU.mult))
                if fetched:
                    dve.tensor_copy(R.soft[:, t - DT], gij[:, 0])
                    dve.scalar_tensor_tensor(R.expert[:, t - DT], gij[:, 1], float(NKEYS), gij[:, 2],
                                             ALU.mult, ALU.add)
                dve.sem_inc(gij_ok, 1)
                assert count[0] == LINKS, count

            def g_low(t, s):
                wait_apart(dve, t_ev, t + 1)
                cols = bass.ds(t * P, P)
                dve.scalar_tensor_tensor(R.g_lo[:, cols], ps[:, s, 0:P], GSCALE, R.g_hi[:, cols], ALU.mult,
                                         ALU.subtract).then_inc(g_lo_ok, 1)
            tiles(dve, tile)
            g_low(TT - 1, (TT - 1) % 2)

        @block.tensor
        def _(pe):
            pe.wait_ge(w_lo_ok, KW)
            pe.wait_ge(p_lo_ok, 1)
            pe.wait_ge(consts, 32)

            def tile(t, s, peeled, _):
                if not peeled:
                    pe.wait_ge(sig, t - 1)
                for (out, hi, lo, k0, n_k) in ((ps_g[:, s], R.h_hi, R.h_lo, 0, KO), (ps_p, p_hi, p_lo, KO, KP)):
                    if k0 == KO and not (isinstance(t, int) and t == 0):
                        pe.wait_ge(prod, t)
                    for k in range(n_k):
                        cols = bass.ds(t * P, P)
                        lhs = hi[:, k, cols], lo[:, k, cols]
                        for half in range(2):
                            n = slice(half * 512, (half + 1) * 512)
                            last = hi_lo(pe, out[:, n], *lhs, w_hi[:, k0 + k, n], w_lo[:, k0 + k, n],
                                         k == 0, k == n_k - 1)
                last.then_inc(e_mm, 1)
                pe.wait_ge(gij_ok, t + 1)
                if not peeled:
                    pe.wait_ge(g_lo_ok, t - 1)
                for a in range(3):
                    last = pe.transpose(ps[:, s, a * P:(a + 1) * P], gij[:, a], ident[:])
                last.then_inc(t_mm, 1)
            tiles(pe, tile)


I_GROUP = 4
N_GROUPS = NKEYS // I_GROUP


def h_rows(R, tile):
    part = R.h_hi if tile < GT // 2 else R.h_lo
    at = ND // 2 + tile % (GT // 2) * (D // KO)
    return part[:].bitcast(f32)[:, :, at:at + D // KO]


def dense_gates(nc, A, R):
    with ExitStack() as c:
        sb = lambda n, s, d: c.enter_context(nc.sbuf_tensor(n, s, d))
        sem = lambda n: R.stack.enter_context(nc.semaphore(n))
        OCT, RING, HALF_T, QUAD = 8, 3, 32, 4
        BODY = 2 * HALF_T
        row = sb("g_row", [P, NKEYS], f32)
        iota = sb("g_iota", [P, NKEYS, OCT], f16)
        hot_i, hot_j = sb("g_hot_i", [P, NKEYS, OCT], f16), sb("g_hot_j", [P, RING, NKEYS, OCT], f16)
        hot_g = sb("g_hot_g", [P, RING, 2, NKEYS, OCT], f16)
        out = sb("g_out", [P, 2, N_GROUPS, HALF_T, I_GROUP], f32)
        ps = c.enter_context(nc.psum_tensor("g_ps", [P, 4, QUAD, NKEYS], f32))
        consts, hot_ok, i_ok, mm, ev = [sem("g_" + n) for n in "consts hot_ok i_ok mm ev".split()]
        stored = [sem("g_stored0"), sem("g_stored1")]
        block = c.enter_context(nc.Block())
        NQ, NO = BODY // QUAD, BODY // OCT
        TURNS = 3
        LOOP = (ND // BODY - 1) // TURNS
        REST = [n for n in range(1 + LOOP * TURNS, ND // BODY)]

        def bodies(eng, body):
            body(0, 0, True)
            with eng.Fori(0, LOOP) as i:
                for r in range(TURNS):
                    body(1 + TURNS * i + r, 1 + r, False)
            for n in REST:
                body(n, n, False)

        @block.sync
        def _(sp):
            sp.dma_start(row[:], A["iota"].rearrange("(a n) -> a n", a=1).to_broadcast([P, NKEYS])).then_inc(consts, 16)

            with sp.Fori(0, ND // BODY) as i:
                for h in range(2):
                    sp.wait_ge(ev, NQ * i + NQ // 2 * (h + 1))
                    dst = R.g_dram[:, :, bass.ds(BODY * i + HALF_T * h, HALF_T)].rearrange("g j t f -> j g (t f)")
                    sp.dma_start(dst, out[:, h].rearrange("p g t f -> p g (t f)")).then_inc(stored[h], 16)
            for h in range(2):
                sp.wait_ge(stored[h], 16 * (ND // BODY))

        @block.vector
        def _(dve):
            dve.wait_ge(consts, 16)
            dve.tensor_copy(iota[:], row[:].rearrange("p (n a) -> p n a", a=1).to_broadcast([P, NKEYS, OCT])
                            ).then_inc(i_ok, 1)
            dve.wait_ge(i_ok, 1)

            def body(n, turn, first):
                for o in range(NO):
                    s = (NO * turn + o) % RING
                    toks = bass.ds(BODY * n + OCT * o, OCT)
                    each = lambda ap: ap.rearrange("p (a t) -> p a t", a=1).to_broadcast([P, NKEYS, OCT])
                    dve.tensor_tensor(hot_i[:], iota[:], each(R.ij[:, 0, toks]), ALU.is_equal).then_inc(i_ok, 1)
                    if not first or o >= RING:
                        dve.wait_ge(mm, 2 * (NO * n + o - RING + 1))
                    dve.tensor_tensor(hot_j[:, s], iota[:], each(R.ij[:, 1, toks]), ALU.is_equal)
                    dve.wait_ge(i_ok, NO * n + o + 2)
                    dve.tensor_tensor(hot_g[:, s, 0], hot_i[:], each(R.g_hi[:, toks]), ALU.mult)
                    dve.tensor_tensor(hot_g[:, s, 1], hot_i[:], each(R.g_lo[:, toks]), ALU.mult).then_inc(hot_ok, 1)
                    dve.wait_ge(hot_ok, NO * n + o + 1)
            bodies(dve, body)

        @block.tensor
        def _(pe):
            def body(n, turn, first):
                for q in range(NQ):
                    o, s = q // 2, (NO * turn + q // 2) % RING
                    if not first or q >= 4:
                        pe.wait_ge(ev, NQ * n + q - 3)
                    if q % 2 == 0:
                        pe.wait_ge(hot_ok, NO * n + o + 1)
                    for u in range(QUAD):
                        t = QUAD * (q % 2) + u
                        pe.matmul(ps[:, q % 4, u], hot_j[:, s, :, t], hot_g[:, s, 0, :, t], start=True, stop=False)
                        last = pe.matmul(ps[:, q % 4, u], hot_j[:, s, :, t], hot_g[:, s, 1, :, t], start=False, stop=True)
                    last.then_inc(mm, 1)
            bodies(pe, body)

        @block.scalar
        def _(act):
            def body(n, turn, first):
                for q in range(NQ):
                    h = q // (NQ // 2)
                    t0 = QUAD * (q % (NQ // 2))
                    if q % (NQ // 2) == 0 and not first:
                        act.wait_ge(stored[h], 16 * n)
                    act.wait_ge(mm, NQ * n + q + 1)
                    act.activation(out[:, h, :, t0:t0 + QUAD].rearrange("p g t f -> p t g f"),
                                   ps[:, q % 4].rearrange("p t (g f) -> p t g f", f=I_GROUP), ACT.Copy).then_inc(ev, 1)
            for tile in range(GT):
                act.activation(h_rows(R, tile), R.h_nat[:, tile].rearrange("p (k c) -> p k c", k=KO), ACT.Copy)
            bodies(act, body)


def experts(nc, A, R):
    with ExitStack() as c:
        sb = lambda n, s, d: c.enter_context(nc.sbuf_tensor(n, s, d))
        sem = lambda n: R.stack.enter_context(nc.semaphore(n))
        E = I_GROUP
        VISITS = GT * P // N_GROUPS
        PER_TILE = P // N_GROUPS
        RING = 4
        NBD = len(DENSE)
        u_st, v_st = sb("x_u_st", [P, 2, D], f32), sb("x_v_st", [P, 2, D], f32)
        u_hi, u_lo = sb("x_u_hi", [P, E, KO, P], f16), sb("x_u_lo", [P, E, KO, P], f16)
        v_hi, v_lo = sb("x_v_hi", [P, E, D], f16), sb("x_v_lo", [P, E, D], f16)
        gate = sb("x_gate", [P, ND, E], f32)
        g_act, w = sb("x_g_act", [P, 2, 512], f32), sb("x_w", [P, 2, 512], f32)
        w_hi, w_lo = sb("x_w_hi", [P, E, ND], f16), sb("x_w_lo", [P, E, ND], f16)
        rows = sb("x_rows", [P, RING, 2 * D], f32)
        index = sb("x_index", [P, RING], u32)
        dots, share = sb("x_dots", [P, 2, 2], f32), sb("x_share", [P, 2], f32)
        ps_a = c.enter_context(nc.psum_tensor("x_ps_a", [P, 4, 512], f32))
        ps_v = c.enter_context(nc.psum_tensor("x_ps_v", [P, 2, D], f32))
        u_in = [sem("x_u_in0"), sem("x_u_in1")]
        v_in = [sem("x_v_in0"), sem("x_v_in1")]
        gate_in = [sem(f"x_gate_in{b}") for b in range(NBD)]
        rows_in = [sem(f"x_rows_in{r}") for r in range(RING)]
        u_hi_ok, u_lo_ok, v_hi_ok, v_lo_ok, a_mm, gelu_ok, w_ok, w_hi_ok, w_lo_ok, v_mm, added = [
            sem("x_" + n) for n in "u_hi_ok u_lo_ok v_hi_ok v_lo_ok a_mm gelu_ok w_ok w_hi_ok w_lo_ok v_mm added".split()]
        dot_ok, alive, share_ok, visited, index_ok = [sem("x_" + n) for n in
            "dot_ok alive share_ok visited index_ok".split()]
        A_STEPS = NBD * E
        V_STEPS = DT
        AT = {("a", k): int(k < E or k % E in (1, 3)) for k in range(A_STEPS)}
        rest = VISITS - sum(AT.values())
        AT.update({("v", t): (t + 1) * rest // DT - t * rest // DT for t in range(DT)})
        assert sum(AT.values()) == VISITS and DT >= E
        block = c.enter_context(nc.Block())
        u_all, v_all, uv_all = A["peer_u_t"], A["peer_v"], A["peer_uv"]

        @block.sync
        def _(sp):
            def load_u(i, e, first=False):
                n = E * i + e
                if not first or e >= 2:
                    sp.wait_ge(u_lo_ok, n - 1)
                sp.dma_start(u_st[:, e % 2], u_all[n]).then_inc(u_in[e % 2], 16)

            def load_v(i, e, first=False):
                n = E * i + e
                if not first or e >= 2:
                    sp.wait_ge(v_lo_ok, n - 1)
                sp.dma_start(v_st[:, e % 2], v_all[n]).then_inc(v_in[e % 2], 16)

            def load_gates(i, b, first=False):
                t0, n_t = DENSE[b]
                if not first:
                    sp.wait_ge(w_ok, A_STEPS * (i - 1) + E * (b + 1))
                sp.dma_start(gate[:, t0:t0 + n_t], R.g_dram[i, :, t0:t0 + n_t]).then_inc(gate_in[b], 16)

            def group(i, first=False):
                for e in range(2, E):
                    load_u(i, e, first)
                for e in range(E):
                    load_v(i, e, first)

            def next_group(i, first=False):
                for e in range(2):
                    load_u(i, e, first)
                for b in range(NBD):
                    load_gates(i, b, first)
            next_group(0, True)
            group(0, True)
            with sp.Fori(1, N_GROUPS) as i:
                next_group(i)
                group(i)

        def visit(i, m):
            return m // PER_TILE, PER_TILE * i + m % PER_TILE

        @block.gpsimd
        def _(pool):
            def group(i, first):
                for m in range(VISITS):
                    tile, hk = visit(i, m)
                    if not first or m >= RING:
                        wait_apart(pool, visited, VISITS * i + m - RING + 1)
                    pool.tensor_copy(index[:, m % RING:m % RING + 1],
                                     R.expert[:, tile, bass.ds(hk, 1)]).then_inc(index_ok, 1)
                    wait_apart(pool, index_ok, VISITS * i + m + 1)
                    pool.indirect_dma_start(rows[:, m % RING], None, uv_all,
                                            bass.IndirectOffsetOnAxis(ap=index[:, m % RING:m % RING + 1], axis=0)
                                            ).then_inc(rows_in[m % RING], 16)
            group(0, True)
            with pool.Fori(1, N_GROUPS) as i:
                group(i, False)

        @block.scalar
        def _(act):
            def u_split(i, e, first=False):
                act.wait_ge(u_in[e % 2], 32 * i + 16 * (e // 2 + 1))
                if not first:
                    act.wait_ge(a_mm, A_STEPS * i - E + e + 1)
                act.activation(u_hi[:, e].rearrange("p a b -> p (a b)"), u_st[:, e % 2], ACT.Copy,
                               scale=WSCALE).then_inc(u_hi_ok, 1)

            def group(i, first, last=False):
                m = [0]

                def visits(place):
                    for _ in range(AT[place]):
                        tile, hk = visit(i, m[0])
                        n, s = VISITS * i + m[0], m[0] % 2
                        act.wait_ge(dot_ok, n + 1)
                        act.activation(dots[:, s, 1:2], dots[:, s, 0:1], ACT.Gelu).then_inc(alive, 1)
                        if not first or m[0] >= 2:
                            act.wait_ge(visited, n - 1)
                        wait_apart(act, alive, n + 1)
                        act.activation(share[:, s:s + 1], dots[:, s, 1:2], ACT.Copy,
                                       scale=R.soft[:, tile, bass.ds(hk, 1)]).then_inc(share_ok, 1)
                        m[0] += 1

                def high(n, slot, e, t0, n_t):
                    act.wait_ge(w_ok, n + 1)
                    act.activation(w_hi[:, e, t0:t0 + n_t], w[:, slot, 0:n_t], ACT.Copy).then_inc(w_hi_ok, 1)
                before = None
                for b, (t0, n_t) in enumerate(DENSE):
                    for e in range(E):
                        k = E * b + e
                        n = A_STEPS * i + k
                        act.wait_ge(a_mm, n + 1)
                        if not first or k >= 2:
                            act.wait_ge(w_ok, n - 1)
                        act.activation(g_act[:, k % 2, 0:n_t], ps_a[:, k % 4, 0:n_t], ACT.Gelu,
                                       scale=1 / WSCALE).then_inc(gelu_ok, 1)
                        if before:
                            high(n - 1, (k - 1) % 2, *before)
                        before = (e, t0, n_t)
                        if b == 0:
                            act.wait_ge(v_in[e % 2], 32 * i + 16 * (e // 2 + 1))
                            if not first:
                                act.wait_ge(v_mm, V_STEPS * i)
                            act.activation(v_hi[:, e], v_st[:, e % 2], ACT.Copy, scale=VSCALE).then_inc(v_hi_ok, 1)
                        visits(("a", k))
                high(n, k % 2, *before)
                for t in range(DT):
                    if t < E and not last:
                        u_split(i + 1, t)
                    visits(("v", t))
            for e in range(E):
                u_split(0, e, True)
            group(0, True)
            with act.Fori(1, N_GROUPS - 1) as i:
                group(i, False)
            group(N_GROUPS - 1, False, True)

        @block.vector
        def _(dve):
            def use(n, s, r, tile):
                dve.wait_ge(share_ok, n + 1)
                dve.scalar_tensor_tensor(R.acc[:, DT + tile], rows[:, r, D:2 * D], share[:, s:s + 1],
                                         R.acc[:, DT + tile], ALU.mult, ALU.add).then_inc(visited, 1)

            def u_split(i, e, _first=False):
                dve.wait_ge(u_hi_ok, E * i + e + 1)
                dve.scalar_tensor_tensor(u_lo[:, e].rearrange("p a b -> p (a b)"), u_st[:, e % 2], WSCALE,
                                         u_hi[:, e].rearrange("p a b -> p (a b)"), ALU.mult,
                                         ALU.subtract).then_inc(u_lo_ok, 1)

            def group(i, first, last=False):
                m = [0]

                def visits(place):
                    for _ in range(AT[place]):
                        k = m[0]
                        tile, _hk = visit(i, k)
                        n = VISITS * i + k
                        dve.wait_ge(rows_in[k % RING], 16 * (VISITS // RING) * i + 16 * (k // RING + 1))
                        dve.tensor_tensor_reduce(out=rows[:, k % RING, 0:D].rearrange("p (k c) -> p k c", k=KO), in0=h_rows(R, tile),
                                                 in1=rows[:, k % RING, 0:D].rearrange("p (k c) -> p k c", k=KO),
                                                 scale=1.0, scalar=0.0, op0=ALU.mult, op1=ALU.add,
                                                 accum_out=dots[:, k % 2, 0:1]).then_inc(dot_ok, 1)
                        if not first or k:
                            if not first or k >= 2:
                                dve.wait_ge(visited, n - 1)
                            use(n - 1, (k - 1) % 2, (k - 1) % RING, visit(i, k - 1)[0] if k else GT - 1)
                        m[0] += 1

                def low(n, slot, e, t0, n_t):
                    dve.wait_ge(w_hi_ok, n + 1)
                    dve.tensor_tensor(w_lo[:, e, t0:t0 + n_t], w[:, slot, 0:n_t], w_hi[:, e, t0:t0 + n_t],
                                      ALU.subtract).then_inc(w_lo_ok, 1)
                before = None
                for b, (t0, n_t) in enumerate(DENSE):
                    dve.wait_ge(gate_in[b], 16 * i + 16)
                    for e in range(E):
                        k = E * b + e
                        n = A_STEPS * i + k
                        dve.wait_ge(gelu_ok, n + 1)
                        if not first or k >= 2:
                            dve.wait_ge(w_lo_ok, n - 1)
                        dve.tensor_tensor(w[:, k % 2, 0:n_t], g_act[:, k % 2, 0:n_t], gate[:, t0:t0 + n_t, e],
                                          ALU.mult).then_inc(w_ok, 1)
                        if before:
                            low(n - 1, (k - 1) % 2, *before)
                        before = (e, t0, n_t)
                        visits(("a", k))
                        if b == 0:
                            dve.wait_ge(v_hi_ok, E * i + e + 1)
                            dve.scalar_tensor_tensor(v_lo[:, e], v_st[:, e % 2], VSCALE, v_hi[:, e], ALU.mult,
                                                     ALU.subtract).then_inc(v_lo_ok, 1)
                low(n, k % 2, *before)
                for t in range(DT):
                    dve.wait_ge(v_mm, V_STEPS * i + t + 1)
                    dve.scalar_tensor_tensor(R.acc[:, t], ps_v[:, t % 2], 1 / (VSCALE * GSCALE), R.acc[:, t],
                                             ALU.mult, ALU.add).then_inc(added, 1)
                    visits(("v", t))
                    if t < E and not last:
                        u_split(i + 1, t)
            for e in range(E):
                u_split(0, e, True)
            group(0, True)
            with dve.Fori(1, N_GROUPS - 1) as i:
                group(i, False)
            group(N_GROUPS - 1, False, True)
            end = N_GROUPS * VISITS - 1
            dve.wait_ge(visited, end)
            use(end, (VISITS - 1) % 2, (VISITS - 1) % RING, GT - 1)

        @block.tensor
        def _(pe):
            def group(i, first):
                def a_block(b):
                    t0, n_t = DENSE[b]
                    t = slice(t0, t0 + n_t)
                    for e in range(E):
                        k = E * b + e
                        n = A_STEPS * i + k
                        out = ps_a[:, k % 4, 0:n_t]
                        if not first or k >= 4:
                            pe.wait_ge(gelu_ok, n - 3)
                        if b == 0:
                            pe.wait_ge(u_hi_ok, E * i + e + 1)
                        for ko in range(KO):
                            pe.matmul(out, u_hi[:, e, ko], R.h_hi[:, ko, t], start=ko == 0, stop=False)
                            pe.matmul(out, u_hi[:, e, ko], R.h_lo[:, ko, t], start=False, stop=False)
                        if b == 0:
                            pe.wait_ge(u_lo_ok, E * i + e + 1)
                        for ko in range(KO):
                            last = pe.matmul(out, u_lo[:, e, ko], R.h_hi[:, ko, t], start=False, stop=ko == KO - 1)
                        last.then_inc(a_mm, 1)

                def v_block(b):
                    t0, n_t = DENSE[b]
                    pe.wait_ge(w_lo_ok, A_STEPS * i + E * (b + 1))
                    if b == 0:
                        pe.wait_ge(v_lo_ok, E * (i + 1))
                    for t in range(t0 // P, (t0 + n_t) // P):
                        if not first or t >= 2:
                            pe.wait_ge(added, V_STEPS * i + (t - 1 if DT % 2 == 0 or t else 0))
                        cols = slice(t * P, (t + 1) * P)
                        for e in range(E):
                            for half in range(2):
                                d = slice(half * 512, (half + 1) * 512)
                                last = hi_lo(pe, ps_v[:, t % 2, d], w_hi[:, e, cols], w_lo[:, e, cols],
                                             v_hi[:, e, d], v_lo[:, e, d], e == 0, e == E - 1)
                        last.then_inc(v_mm, 1)
                for b in range(NBD):
                    a_block(b)
                for b in range(NBD):
                    v_block(b)
            group(0, True)
            with pe.Fori(1, N_GROUPS) as i:
                group(i, False)


def final_norm(nc, A, R, outs):
    with ExitStack() as c:
        sb = lambda n, s, d: c.enter_context(nc.sbuf_tensor(n, s, d))
        sem = lambda n: R.stack.enter_context(nc.semaphore(n))
        gain, shift = sb("n_gain", [P, D], f32), sb("n_shift", [P, D], f32)
        stats, mv = sb("n_stats", [P, 2, 2, 6], f32), sb("n_mv", [P, 2, 4], f32)
        consts, v_ok, sq_ok, scaled, y_ok, dve_in, stored = [sem("n_" + n) for n in
            "consts v_ok sq_ok scaled y_ok dve_in stored".split()]
        block = c.enter_context(nc.Block())

        @block.sync
        def _(sp):
            sp.dma_start(gain[:], A["ln2_g"].to_broadcast([P, D])).then_inc(consts, 16)
            sp.dma_start(shift[:], A["ln2_b"].to_broadcast([P, D])).then_inc(consts, 16)
            for t in range(TT):
                sp.wait_ge(y_ok, t + 1)
                k = t * P
                dst = outs[0][0, k:k + P] if k < SEQS[0] else outs[1][0, k - SEQS[0]:k - SEQS[0] + P]
                sp.dma_start(dst, R.acc[:, t]).then_inc(stored, 16)
            sp.wait_ge(stored, 16 * TT)

        @block.scalar
        def _(act):
            for t in range(TT):
                act.wait_ge(v_ok, t + 1)
                act.activation(mv[:, t % 2, 2:3], mv[:, t % 2, 2:3], ACT.Sqrt).then_inc(sq_ok, 1)

        @block.gpsimd
        def _(pool):
            pool.wait_ge(consts, 32)
            for t in range(TT):
                pool.wait_ge(scaled, t + 1)
                pool.tensor_tensor(R.acc[:, t], R.acc[:, t], shift[:], ALU.add).then_inc(y_ok, 1)

        @block.vector
        def _(dve):
            link = linker(dve, dve_in)

            def statistics(t):
                s = t % 2
                for half in range(2):
                    last = dve.bn_stats(stats[:, s, half], R.acc[:, t, half * 512:(half + 1) * 512])
                link(last)
                link(dve.bn_aggr(mv[:, s, 0:2], stats[:, s].rearrange("p a b -> p (a b)")))
                dve.tensor_scalar(mv[:, s, 2:3], mv[:, s, 1:2], LN_EPS, None, ALU.add).then_inc(v_ok, 1)

            def normalise(t):
                s = t % 2
                dve.wait_ge(sq_ok, t + 1)
                link(dve.reciprocal(mv[:, s, 3:4], mv[:, s, 2:3]))
                link(dve.tensor_scalar(R.acc[:, t], R.acc[:, t], mv[:, s, 0:1], mv[:, s, 3:4], ALU.subtract, ALU.mult))
                dve.tensor_tensor(R.acc[:, t], R.acc[:, t], gain[:], ALU.mult).then_inc(scaled, 1)
            statistics(0)
            dve.wait_ge(consts, 32)
            for t in range(TT):
                if t + 1 < TT:
                    statistics(t + 1)
                normalise(t)


def build(nc, A, outs):
    R = Buffers()
    R.stack = ExitStack()
    with R.stack:
        R.x_hi_dram = nc.dram_tensor("x_hi_scratch", [P, KO, NT], f16).ap()
        R.x_lo_dram = nc.dram_tensor("x_lo_scratch", [P, KO, NT], f16).ap()
        R.g_dram = nc.dram_tensor("gate_scratch", [N_GROUPS, P, ND, I_GROUP], f32).ap()
        with ExitStack() as branches:
            right = lambda n, s, d: branches.enter_context(nc.sbuf_tensor(n, s, d, side="right"))
            with ExitStack() as inputs:
                left = lambda n, s, d: inputs.enter_context(nc.sbuf_tensor(n, s, d))
                R.proj = left("proj", [P, NM, NT], f32)
                values = ExitStack()
                R.v = values.enter_context(nc.sbuf_tensor("v", [P, TT, HEADS * DV], f32))
                project(nc, A, R)
                R.o_hi, R.o_lo = right("o_hi", [P, HEADS, NT], f16), right("o_lo", [P, HEADS, NT], f16)
                gated_attention(nc, A, R)
                values.close()
                R.f_hi, R.f_lo = right("f_hi", [P, GROUPS, NT], f16), right("f_lo", [P, GROUPS, NT], f16)
                fourier(nc, A, R)
            merged = ExitStack()
            R.m_hi = merged.enter_context(nc.sbuf_tensor("m_hi", [P, KO, NT], f16))
            R.m_lo = merged.enter_context(nc.sbuf_tensor("m_lo", [P, KO, NT], f16))
            merge(nc, A, R)
        with ExitStack() as tail:
            right = lambda n, s, d: tail.enter_context(nc.sbuf_tensor(n, s, d, side="right"))
            R.h_hi, R.h_lo = right("h_hi", [P, KO, NT], f16), right("h_lo", [P, KO, NT], f16)
            R.acc = right("acc", [P, TT, D], f32)
            R.expert, R.soft = right("expert", [P, GT, P], u32), right("soft", [P, GT, P], f32)
            rows = ExitStack()
            R.h_nat = rows.enter_context(nc.sbuf_tensor("h_nat", [P, GT, D], f32, side="right"))
            mix_norm(nc, A, R)
            merged.close()
            with ExitStack() as routing:
                routed = lambda n, s: routing.enter_context(nc.sbuf_tensor(n, s, f16, side="right"))
                R.ij, R.g_hi, R.g_lo = routed("ij", [P, 2, NT]), routed("g_hi", [P, NT]), routed("g_lo", [P, NT])
                with ExitStack() as tops:
                    R.top_v = tops.enter_context(nc.sbuf_tensor("top_v", [P, HP, TT, TOPK], f32))
                    R.top_i = tops.enter_context(nc.sbuf_tensor("top_i", [P, HP, TT, TOPK], f16))
                    best_keys(nc, A, R)
                    best_pairs(nc, A, R)
                dense_gates(nc, A, R)
            rows.close()
            experts(nc, A, R)
            final_norm(nc, A, R, outs)


def _halves(table):
    hi = (table * WSCALE).astype(np.float16)
    return hi, (table * WSCALE - hi.astype(np.float64)).astype(np.float16)


def _dft(n):
    k = np.arange(n)
    angle = 2 * np.pi * (np.outer(k, k) % n) / n
    return np.cos(angle), np.sin(angle)


def _tables():
    cos_c, sin_c = _dft(GDIM)
    t = {"dft_c": np.stack(_halves(np.concatenate([cos_c, sin_c], 1)), 1)}
    for name, n in (("dft_t", SEQS[0]), ("dft_s", SEQS[1])):
        cos_t, sin_t = _dft(n)
        parts = np.stack([np.stack(_halves(cos_t)), np.stack(_halves(-sin_t))])
        t[name] = np.ascontiguousarray(parts.reshape(2, 2, n // P, P, n).transpose(3, 0, 1, 2, 4))
    s, q = np.arange(P)[:, None], np.arange(P)[None, :]
    same = s // CHUNK == q // CHUNK
    t["causal"] = np.stack([same & (s <= q), same & (s > q)], 1).astype(np.float32)
    t["ident"] = np.eye(P, dtype=np.float32)
    t["iota"] = np.arange(NKEYS, dtype=np.float32)
    return t


def _column_tiles(w):
    k, n = w.shape
    return np.ascontiguousarray(w.reshape(k // P, P, n // P, P).transpose(2, 1, 0, 3).reshape(n // P, P, k))


def _layout(x):
    a = {k: np.asarray(v) for k, v in x.items()}
    L = _tables()
    tokens = np.concatenate([a["x_prompt"][0], a["x_sample"][0]], 0)
    L["x"] = tokens.reshape(TT, P, D)
    L["x_t"] = np.ascontiguousarray(tokens.T).reshape(KO, P, NT)
    p = np.concatenate([a["p_prompt"][0, 0], a["p_sample"][0, 0]], 0)
    L["p_t"] = np.ascontiguousarray(p.T.reshape(PLE // P, P, NT).transpose(1, 0, 2))
    w = a["w_in"][0]
    qk, vw = HEADS * DK, HEADS * DV
    q, k, v, r = w[:, :qk], w[:, qk:2 * qk], w[:, 2 * qk:2 * qk + vw], w[:, 2 * qk + vw:2 * qk + 2 * vw]
    low = w[:, 2 * qk + 2 * vw:2 * qk + 2 * vw + 2 * RANK]
    f = w[:, 2 * qk + 2 * vw + 2 * RANK:]
    rest = np.zeros((D, P), np.float32)
    rest[:, 0:RANK], rest[:, AB_ROW:AB_ROW + RANK] = low[:, :RANK], low[:, RANK:]
    L["w_proj"] = _column_tiles(np.concatenate([rest, q, k, r, f], 1))
    L["w_v"] = np.ascontiguousarray(v.reshape(4, 2, P, vw).transpose(0, 2, 1, 3).reshape(4, P, 2 * vw))
    a2 = np.zeros((2 * AB_ROW, qk), np.float32)
    a2[0:RANK], a2[AB_ROW:AB_ROW + RANK] = a["w_af2"][0], a["w_ab2"][0]
    L["w_a2"] = a2
    L["b_a"] = np.ascontiguousarray(np.stack([a["b_af"][0].reshape(PAIRS, P), a["b_ab"][0].reshape(PAIRS, P)], 1)
                                    .reshape(2 * PAIRS, P).T)
    L["norm_g"] = a["gla_norm_g"][0].reshape(P, 1)
    mg = _column_tiles(a["w_mg"][0])
    L["w_merge"] = np.concatenate([mg[:KO], mg[KO:], _column_tiles(a["w_ao"][0]), _column_tiles(a["w_fo"][0])], 2)
    L["b_mg"] = np.ascontiguousarray(a["b_mg"][0].reshape(2, KO, P).transpose(2, 0, 1))
    L["w_o"] = a["w_o"][0].reshape(KO, P, D)
    L["w_ple"] = np.concatenate([a["w_pg"][0].reshape(KO, P, D), a["w_pe"][0].reshape(PLE // P, P, D)], 0)
    keys = a["peer_keys"][0].reshape(HP, NKEYS, HALF).transpose(0, 2, 1)
    L["w_route"] = np.concatenate([_column_tiles(a["w_pq"][0]), keys], 2)
    L["peer_u_t"] = _column_tiles(np.ascontiguousarray(a["peer_u"][0].T))
    L["peer_v"] = a["peer_v"][0].reshape(EXPERTS // P, P, D)
    L["peer_uv"] = np.concatenate([a["peer_u"][0], a["peer_v"][0]], 1)
    for n in ("ln1_g", "ln1_b", "ln2_g", "ln2_b"):
        L[n] = a[n][0].reshape(1, D)
    return L


def kernel(**inputs):
    import concourse.bacc as bacc
    from concourse.bass_utils import run_bass_kernel_spmd

    nc = bacc.Bacc("TRN2", target_bir_lowering=False, num_devices=1)
    arrays = {n: np.ascontiguousarray(a) for n, a in _layout(inputs).items()}
    A = {n: nc.dram_tensor("in_" + n, a.shape, mybir.dt.from_np(a.dtype), kind="ExternalInput").ap()
         for n, a in arrays.items()}
    outs = [nc.dram_tensor(f"out_{i}", (1, n, D), f32, kind="ExternalOutput").ap() for i, n in enumerate(SEQS)]
    build(nc, A, outs)
    r = run_bass_kernel_spmd(nc, [{"in_" + n: a for n, a in arrays.items()}], core_ids=[0])
    return r.results[0]["out_0"], r.results[0]["out_1"]
```
